# Optimizing a Trainium2 kernel written in Bass

```python
import math
import jax, jax.numpy as jnp
from jax import lax
import numpy as np

D_MODEL = 1024
BATCH = 1
SEQ = 256
DEPTH = 2

N_A_LAYERS = max(1, DEPTH // 2)
N_B_LAYERS = DEPTH - N_A_LAYERS

A_HEADS = D_MODEL // 128
A_HEAD_DIM = 64
A_V_DIM = 2 * A_HEAD_DIM
A_QK_WIDTH = A_HEADS * 2 * A_HEAD_DIM
A_V_WIDTH = A_HEADS * A_V_DIM
LAMBDA_INIT_BASE = 0.8
LAMBDA_INIT_AMP = 0.6
LAMBDA_INIT_RATE = 0.3

ROPE_THETA = 500000.0
ROT_DIM = A_HEAD_DIM // 4

B_HEADS = D_MODEL // 64
B_HEAD_DIM = 64
B_WIDTH = B_HEADS * B_HEAD_DIM

D_FF = -(-8 * D_MODEL // (3 * 256)) * 256

Q_BLOCK = 128
EPS = 1e-6


def rms_norm(x, g):
    x32 = x.astype(jnp.float32)
    y = x32 * lax.rsqrt(jnp.mean(x32 * x32, axis=-1, keepdims=True) + EPS)
    return (y * g.astype(jnp.float32)).astype(x.dtype)

def rope_tables(seq):
    pos = jnp.arange(seq, dtype=jnp.float32)
    inv_freq = ROPE_THETA ** (-jnp.arange(0, ROT_DIM, 2, dtype=jnp.float32) / ROT_DIM)
    ang = pos[:, None] * inv_freq[None, :]
    return jnp.cos(ang), jnp.sin(ang)

def apply_partial_rope(t, cos, sin):
    half = ROT_DIM // 2
    t1 = t[..., :half].astype(jnp.float32)
    t2 = t[..., half:ROT_DIM].astype(jnp.float32)
    r1 = t1 * cos - t2 * sin
    r2 = t2 * cos + t1 * sin
    return jnp.concatenate([r1.astype(t.dtype), r2.astype(t.dtype), t[..., ROT_DIM:]], axis=-1)

def to_blocks(t):
    b, h, s, d = t.shape
    return t.reshape(b, h, s // Q_BLOCK, Q_BLOCK, d).transpose(2, 0, 1, 3, 4)

def from_blocks(o):
    nb, b, h, qb, d = o.shape
    return o.transpose(1, 0, 3, 2, 4).reshape(b, nb * qb, h, d)

def diff_attention(h, w_qkv, w_o, lq1, lk1, lq2, lk2, subln_g, lambda_init, cos, sin):
    b, s, _ = h.shape
    qkv = h @ w_qkv
    q, k, v = jnp.split(qkv, [A_QK_WIDTH, 2 * A_QK_WIDTH], axis=-1)
    q = q.reshape(b, s, 2 * A_HEADS, A_HEAD_DIM).transpose(0, 2, 1, 3)
    k = k.reshape(b, s, 2 * A_HEADS, A_HEAD_DIM).transpose(0, 2, 1, 3)
    v = v.reshape(b, s, A_HEADS, A_V_DIM).transpose(0, 2, 1, 3)
    q = apply_partial_rope(q, cos, sin)
    k = apply_partial_rope(k, cos, sin)
    f32 = jnp.float32
    lam = (jnp.exp(jnp.sum(lq1.astype(f32) * lk1.astype(f32)))
           - jnp.exp(jnp.sum(lq2.astype(f32) * lk2.astype(f32))) + lambda_init)
    scale = A_HEAD_DIM ** -0.5
    kpos = jnp.arange(s)
    n_blocks = s // Q_BLOCK

    def block(args):
        qb, start = args
        sc = jnp.einsum('bhqd,bhkd->bhqk', qb, k).astype(f32) * scale
        qpos = start + jnp.arange(Q_BLOCK)
        mask = kpos[None, :] <= qpos[:, None]
        p = jax.nn.softmax(jnp.where(mask, sc, -jnp.inf), axis=-1)
        p = p.reshape(b, A_HEADS, 2, Q_BLOCK, s)
        a = p[:, :, 0] - lam * p[:, :, 1]
        return jnp.einsum('bhqk,bhkd->bhqd', a.astype(v.dtype), v)

    o = lax.map(block, (to_blocks(q), jnp.arange(n_blocks) * Q_BLOCK))
    o = from_blocks(o)
    o = rms_norm(o, subln_g) * (1.0 - lambda_init)
    return o.reshape(b, s, A_V_WIDTH).astype(h.dtype) @ w_o

def stick_breaking_attention(h, w_q, w_o, k, v):
    b, s, _ = h.shape
    q = (h @ w_q).reshape(b, s, B_HEADS, B_HEAD_DIM).transpose(0, 2, 1, 3)
    f32 = jnp.float32
    scale = B_HEAD_DIM ** -0.5
    kpos = jnp.arange(s)
    n_blocks = s // Q_BLOCK

    def block(args):
        qb, start = args
        z = jnp.einsum('bhqd,bhkd->bhqk', qb, k).astype(f32) * scale
        qpos = start + jnp.arange(Q_BLOCK)
        mask = kpos[None, :] < qpos[:, None]
        log_beta = jax.nn.log_sigmoid(z)
        log_1m = jnp.where(mask, jax.nn.log_sigmoid(-z), 0.0)
        between = lax.cumsum(log_1m, axis=3, reverse=True) - log_1m
        a = jnp.where(mask, jnp.exp(log_beta + between), 0.0)
        return jnp.einsum('bhqk,bhkd->bhqd', a.astype(v.dtype), v)

    o = lax.map(block, (to_blocks(q), jnp.arange(n_blocks) * Q_BLOCK))
    o = from_blocks(o).reshape(b, s, B_WIDTH)
    return o @ w_o

def swiglu(h, w_gate_up, w_down):
    gate, up = jnp.split(h @ w_gate_up, 2, axis=-1)
    return (jax.nn.silu(gate) * up) @ w_down

def first_inputs(seed: int = 0) -> dict:
    key = jax.random.key(seed)
    ks = jax.random.split(key, 24)
    f32 = jnp.float32

    def w(k, shape, fan_in):
        return jax.random.normal(k, shape, f32) * (fan_in ** -0.5)

    def gain(k, shape):
        return 1.0 + 0.02 * jax.random.normal(k, shape, f32)

    return {
        'x': jax.random.normal(ks[0], (BATCH, SEQ, D_MODEL), f32),
        'a_w_qkv': w(ks[1], (N_A_LAYERS, D_MODEL, 2 * A_QK_WIDTH + A_V_WIDTH), D_MODEL),
        'a_w_o': w(ks[2], (N_A_LAYERS, A_V_WIDTH, D_MODEL), A_V_WIDTH),
        'a_lambda_q1': 0.1 * jax.random.normal(ks[3], (N_A_LAYERS, A_HEAD_DIM), f32),
        'a_lambda_k1': 0.1 * jax.random.normal(ks[4], (N_A_LAYERS, A_HEAD_DIM), f32),
        'a_lambda_q2': 0.1 * jax.random.normal(ks[5], (N_A_LAYERS, A_HEAD_DIM), f32),
        'a_lambda_k2': 0.1 * jax.random.normal(ks[6], (N_A_LAYERS, A_HEAD_DIM), f32),
        'a_subln_g': gain(ks[7], (N_A_LAYERS, A_V_DIM)),
        'kv_norm_g': gain(ks[8], (D_MODEL,)),
        'kv_w': w(ks[9], (D_MODEL, 2 * B_WIDTH), D_MODEL),
        'b_w_q': w(ks[10], (N_B_LAYERS, D_MODEL, B_WIDTH), D_MODEL),
        'b_w_o': w(ks[11], (N_B_LAYERS, B_WIDTH, D_MODEL), B_WIDTH),
        'mix_pre_g': gain(ks[12], (DEPTH, D_MODEL)),
        'mix_post_g': gain(ks[13], (DEPTH, D_MODEL)),
        'ffn_pre_g': gain(ks[14], (DEPTH, D_MODEL)),
        'ffn_post_g': gain(ks[15], (DEPTH, D_MODEL)),
        'ffn_w_gate_up': w(ks[16], (DEPTH, D_MODEL, 2 * D_FF), D_MODEL),
        'ffn_w_down': w(ks[17], (DEPTH, D_FF, D_MODEL), D_FF),
    }

def first_block(x, a_w_qkv, a_w_o, a_lambda_q1, a_lambda_k1, a_lambda_q2, a_lambda_k2,
              a_subln_g, kv_norm_g, kv_w, b_w_q, b_w_o, mix_pre_g, mix_post_g,
              ffn_pre_g, ffn_post_g, ffn_w_gate_up, ffn_w_down):
    b, s, _ = x.shape
    cos, sin = rope_tables(s)
    shared_k = None
    shared_v = None
    for layer in range(DEPTH):
        h = rms_norm(x, mix_pre_g[layer])
        if layer < N_A_LAYERS:
            lambda_init = LAMBDA_INIT_BASE - LAMBDA_INIT_AMP * math.exp(-LAMBDA_INIT_RATE * layer)
            m = diff_attention(h, a_w_qkv[layer], a_w_o[layer],
                               a_lambda_q1[layer], a_lambda_k1[layer],
                               a_lambda_q2[layer], a_lambda_k2[layer],
                               a_subln_g[layer], lambda_init, cos, sin)
        else:
            if shared_k is None:
                kv = rms_norm(x, kv_norm_g) @ kv_w
                kk, vv = jnp.split(kv, 2, axis=-1)
                shared_k = kk.reshape(b, s, B_HEADS, B_HEAD_DIM).transpose(0, 2, 1, 3)
                shared_v = vv.reshape(b, s, B_HEADS, B_HEAD_DIM).transpose(0, 2, 1, 3)
            j = layer - N_A_LAYERS
            m = stick_breaking_attention(h, b_w_q[j], b_w_o[j], shared_k, shared_v)
        x = x + rms_norm(m, mix_post_g[layer])
        f = swiglu(rms_norm(x, ffn_pre_g[layer]), ffn_w_gate_up[layer], ffn_w_down[layer])
        x = x + rms_norm(f, ffn_post_g[layer])
    return x


DEPTH_2 = 1

GRID_W = 64
CTX_LEN = 256
N_HEADS_M = 4
D_MLSTM = 1024
HEAD_DIM_M = D_MLSTM // N_HEADS_M
MLSTM_CHUNK = 128
CONV_W = 3
N_GROUPS_S = 4
D_SGU = 1024
GROUP_DIM_S = D_SGU // N_GROUPS_S
SGU_CHUNK = 128
D_FF_2 = 2816
N_MOD = 9
POS_BASE = 10000.0
F_BIAS_LO = 3.0
F_BIAS_HI = 6.0
PROJ_SIZES = (D_MLSTM, D_MLSTM, D_MLSTM, 4 * N_HEADS_M, D_MLSTM, D_SGU, D_SGU, D_MODEL, D_MODEL)
N_STATE_PIECES = 4
D_PROJ = sum(PROJ_SIZES)


def rmsnorm(x, g):
    x32 = x.astype(jnp.float32)
    y = x32 * lax.rsqrt(jnp.mean(x32 * x32, axis=-1, keepdims=True) + EPS)
    return (y * g.astype(jnp.float32)).astype(x.dtype)

def modulate(x, shift, scale):
    return x * (1.0 + scale[:, None, :]) + shift[:, None, :]

def ffn_sublayer(h, shift, scale, gate, g, w_in, w_out):
    hn = modulate(rmsnorm(h, g), shift, scale)
    a, b = jnp.split(hn @ w_in, 2, axis=-1)
    y = (jax.nn.silu(a) * b) @ w_out
    return h + 0.5 * gate[:, None, :] * y

def grid_pos_emb(rows):
    t = jnp.arange(rows * GRID_W)
    r = (t // GRID_W).astype(jnp.float32)
    col = (t % GRID_W).astype(jnp.float32)
    quarter = D_MODEL // 4
    freqs = jnp.exp(-math.log(POS_BASE) * jnp.arange(quarter, dtype=jnp.float32) / quarter)
    ar = r[:, None] * freqs
    ac = col[:, None] * freqs
    return jnp.concatenate([jnp.sin(ar), jnp.cos(ar), jnp.sin(ac), jnp.cos(ac)], axis=-1)

def split_cols(p, sizes):
    out = []
    off = 0
    for s in sizes:
        out.append(p[..., off:off + s])
        off += s
    return out

def project(h, shift, scale, g, w_in, sizes):
    hn = modulate(rmsnorm(h, g), shift, scale)
    return split_cols(hn @ w_in[:, :sum(sizes)], sizes)

def short_conv(x, w, b):
    pad = CONV_W // 2
    s = x.shape[1]
    xp = jnp.pad(x, ((0, 0), (pad, pad), (0, 0)))
    return sum(xp[:, j:j + s] * w[j] for j in range(CONV_W)) + b

def to_heads(t):
    b, s, _ = t.shape
    return t.reshape(b, s, N_HEADS_M, HEAD_DIM_M).transpose(0, 2, 1, 3).astype(jnp.float32)

def mlstm_prep(q, k, v, gates, conv_w, conv_b, b_gates):
    qk = jax.nn.silu(short_conv(jnp.concatenate([q, k], axis=-1), conv_w, conv_b))
    q, k = jnp.split(qk, 2, axis=-1)
    q = to_heads(q) * HEAD_DIM_M ** -0.5
    k = to_heads(k)
    v = to_heads(v)
    gt = jnp.moveaxis((gates + b_gates).astype(jnp.float32), -1, 1)
    nh = N_HEADS_M
    fwd = (gt[:, :nh], jax.nn.log_sigmoid(gt[:, nh:2 * nh]))
    bwd = (gt[:, 2 * nh:3 * nh], jax.nn.log_sigmoid(gt[:, 3 * nh:]))
    return q, k, v, fwd, bwd

def zero_state(bsz):
    return (jnp.zeros((bsz, N_HEADS_M, HEAD_DIM_M, HEAD_DIM_M), jnp.float32),
            jnp.zeros((bsz, N_HEADS_M, HEAD_DIM_M), jnp.float32),
            jnp.zeros((bsz, N_HEADS_M), jnp.float32))

def mlstm_scan(q, k, v, li, lf, state, reverse, emit):
    if reverse:
        q, k, v = jnp.flip(q, 2), jnp.flip(k, 2), jnp.flip(v, 2)
        li, lf = jnp.flip(li, 2), jnp.flip(lf, 2)
    bsz, nh, s, dh = q.shape
    nc = s // MLSTM_CHUNK

    def to_chunks(t):
        return jnp.moveaxis(t.reshape(t.shape[:2] + (nc, MLSTM_CHUNK) + t.shape[3:]), 2, 0)

    tri = jnp.tril(jnp.ones((MLSTM_CHUNK, MLSTM_CHUNK), dtype=bool))

    def body(carry, xs):
        c_st, n_st, m_st = carry
        qc, kc, vc, lic, lfc = xs
        b = jnp.cumsum(lfc, axis=-1)
        g = b[..., -1]
        w = g[..., None] - b + lic
        m_new = jnp.maximum(g + m_st, jnp.max(w, axis=-1))
        ws = jnp.exp(w - m_new[..., None])
        decay = jnp.exp(g + m_st - m_new)
        c_new = decay[..., None, None] * c_st + jnp.einsum('bhsv,bhsk->bhvk', vc * ws[..., None], kc)
        n_new = decay[..., None] * n_st + jnp.einsum('bhs,bhsk->bhk', ws, kc)
        if not emit:
            return (c_new, n_new, m_new), None
        dm = b[..., :, None] - b[..., None, :] + lic[..., None, :]
        dm = jnp.where(tri, dm, -jnp.inf)
        a = b + m_st[..., None]
        m_t = jnp.maximum(a, jnp.max(dm, axis=-1))
        s_ts = jnp.einsum('bhtk,bhsk->bhts', qc, kc) * jnp.exp(dm - m_t[..., None])
        inter = jnp.exp(a - m_t)
        num = jnp.einsum('bhts,bhsv->bhtv', s_ts, vc) + inter[..., None] * jnp.einsum('bhvk,bhtk->bhtv', c_st, qc)
        den = jnp.sum(s_ts, axis=-1) + inter * jnp.einsum('bhk,bhtk->bht', n_st, qc)
        h = num / jnp.maximum(jnp.abs(den), jnp.exp(-m_t))[..., None]
        return (c_new, n_new, m_new), h

    state, hs = lax.scan(body, state, (to_chunks(q), to_chunks(k), to_chunks(v), to_chunks(li), to_chunks(lf)))
    if not emit:
        return None, state
    h = jnp.moveaxis(hs, 0, 2).reshape(bsz, nh, s, dh)
    if reverse:
        h = jnp.flip(h, 2)
    return h, state

def head_layernorm(h, g):
    mu = jnp.mean(h, axis=-1, keepdims=True)
    hc = h - mu
    y = hc * lax.rsqrt(jnp.mean(hc * hc, axis=-1, keepdims=True) + EPS)
    bsz, nh, s, dh = h.shape
    return y.transpose(0, 2, 1, 3).reshape(bsz, s, nh * dh) * g.astype(jnp.float32)

def spatial_gating(u, v, g, w_s, b_s):
    bsz, s, _ = v.shape
    nc = s // SGU_CHUNK
    vn = rmsnorm(v, g).reshape(bsz, nc, SGU_CHUNK, N_GROUPS_S, GROUP_DIM_S)
    mixed = jnp.einsum('gts,bnsgc->bntgc', w_s, vn) + jnp.swapaxes(b_s, 0, 1)[:, :, None]
    return u * mixed.reshape(bsz, s, D_SGU)

def merge_branches(pieces, h_m, g_head, g_sgu, w_s, b_s, w_a, w_b, w_o):
    o, u, vs, ga, gb = pieces
    y_a = jax.nn.sigmoid(o) * head_layernorm(h_m, g_head).astype(o.dtype)
    y_b = spatial_gating(jax.nn.gelu(u), jax.nn.gelu(vs), g_sgu, w_s, b_s)
    mixed = jax.nn.sigmoid(ga) * (y_a @ w_a) + jax.nn.sigmoid(gb) * (y_b @ w_b)
    return mixed @ w_o

def second_inputs(seed: int = 0) -> dict:
    key = jax.random.key(seed)
    ks = jax.random.split(key, 28)
    f32 = jnp.float32
    L = DEPTH_2

    def nrm(k, shape, s):
        return jax.random.normal(k, shape, f32) * s

    def gain(k, shape):
        return 1.0 + 0.05 * jax.random.normal(k, shape, f32)

    i_bias = nrm(ks[10], (L, 2, N_HEADS_M), 0.1)
    f_bias = jnp.linspace(F_BIAS_LO, F_BIAS_HI, N_HEADS_M, dtype=f32) + nrm(ks[11], (L, 2, N_HEADS_M), 0.1)
    return {
        'x': nrm(ks[0], (BATCH, SEQ, D_MODEL), 1.0),
        'c': nrm(ks[1], (BATCH, D_MODEL), 1.0),
        'ctx': nrm(ks[2], (BATCH, CTX_LEN, D_MODEL), 1.0),
        'c_ctx': nrm(ks[3], (D_MODEL,), 1.0),
        'w_ada': nrm(ks[4], (L, D_MODEL, N_MOD * D_MODEL), 0.5 * D_MODEL ** -0.5),
        'b_ada': nrm(ks[5], (L, N_MOD * D_MODEL), 0.01),
        'g_ffn1': gain(ks[6], (L, D_MODEL)),
        'w_ffn1_in': nrm(ks[7], (L, D_MODEL, 2 * D_FF_2), D_MODEL ** -0.5),
        'w_ffn1_out': nrm(ks[8], (L, D_FF_2, D_MODEL), D_FF_2 ** -0.5),
        'g_mix': gain(ks[9], (L, D_MODEL)),
        'w_in': nrm(ks[12], (L, D_MODEL, D_PROJ), D_MODEL ** -0.5),
        'b_gates': jnp.stack([i_bias, f_bias], axis=2).reshape(L, 4 * N_HEADS_M),
        'conv_qk_w': nrm(ks[13], (L, CONV_W, 2 * D_MLSTM), CONV_W ** -0.5),
        'conv_qk_b': nrm(ks[14], (L, 2 * D_MLSTM), 0.01),
        'g_head': gain(ks[15], (L, D_MLSTM)),
        'g_sgu': gain(ks[16], (L, D_SGU)),
        'w_s': nrm(ks[17], (L, N_GROUPS_S, SGU_CHUNK, SGU_CHUNK), SGU_CHUNK ** -0.5),
        'b_s': 1.0 + nrm(ks[18], (L, N_GROUPS_S, SGU_CHUNK), 0.1),
        'w_branch_a': nrm(ks[19], (L, D_MLSTM, D_MODEL), D_MLSTM ** -0.5),
        'w_branch_b': nrm(ks[20], (L, D_SGU, D_MODEL), D_SGU ** -0.5),
        'w_out': nrm(ks[21], (L, D_MODEL, D_MODEL), D_MODEL ** -0.5),
        'g_ffn2': gain(ks[22], (L, D_MODEL)),
        'w_ffn2_in': nrm(ks[23], (L, D_MODEL, 2 * D_FF_2), D_MODEL ** -0.5),
        'w_ffn2_out': nrm(ks[24], (L, D_FF_2, D_MODEL), D_FF_2 ** -0.5),
        'g_final': gain(ks[25], (D_MODEL,)),
    }

def second_block(x, c, ctx, c_ctx, w_ada, b_ada, g_ffn1, w_ffn1_in, w_ffn1_out, g_mix, w_in, b_gates,
              conv_qk_w, conv_qk_b, g_head, g_sgu, w_s, b_s, w_branch_a, w_branch_b, w_out,
              g_ffn2, w_ffn2_in, w_ffn2_out, g_final):
    rows = x.shape[1] // GRID_W
    bsz = x.shape[0]
    h = x + grid_pos_emb(rows).astype(x.dtype)[None]
    hc = ctx
    for layer in range(DEPTH_2):
        is_last = layer == DEPTH_2 - 1
        mods = jnp.split(jax.nn.silu(c) @ w_ada[layer] + b_ada[layer], N_MOD, axis=-1)
        mods_c = jnp.split(jax.nn.silu(c_ctx)[None] @ w_ada[layer] + b_ada[layer], N_MOD, axis=-1)

        h = ffn_sublayer(h, mods[0], mods[1], mods[2], g_ffn1[layer], w_ffn1_in[layer], w_ffn1_out[layer])
        hc = ffn_sublayer(hc, mods_c[0], mods_c[1], mods_c[2], g_ffn1[layer], w_ffn1_in[layer], w_ffn1_out[layer])

        p_lat = project(h, mods[3], mods[4], g_mix[layer], w_in[layer], PROJ_SIZES)
        ctx_sizes = PROJ_SIZES[:N_STATE_PIECES] if is_last else PROJ_SIZES
        p_ctx = project(hc, mods_c[3], mods_c[4], g_mix[layer], w_in[layer], ctx_sizes)
        q_l, k_l, v_l, gf_l, gb_l = mlstm_prep(*p_lat[:N_STATE_PIECES], conv_qk_w[layer], conv_qk_b[layer], b_gates[layer])
        q_c, k_c, v_c, gf_c, gb_c = mlstm_prep(*p_ctx[:N_STATE_PIECES], conv_qk_w[layer], conv_qk_b[layer], b_gates[layer])

        state0 = zero_state(bsz)
        hcf, st_f = mlstm_scan(q_c, k_c, v_c, gf_c[0], gf_c[1], state0, False, not is_last)
        hcb, st_b = mlstm_scan(q_c, k_c, v_c, gb_c[0], gb_c[1], state0, True, not is_last)
        hlf, _ = mlstm_scan(q_l, k_l, v_l, gf_l[0], gf_l[1], st_f, False, True)
        hlb, _ = mlstm_scan(q_l, k_l, v_l, gb_l[0], gb_l[1], st_b, True, True)

        y_lat = merge_branches(p_lat[N_STATE_PIECES:], hlf + hlb, g_head[layer], g_sgu[layer], w_s[layer], b_s[layer],
                               w_branch_a[layer], w_branch_b[layer], w_out[layer])
        h = h + mods[5][:, None, :] * y_lat
        if not is_last:
            y_ctx = merge_branches(p_ctx[N_STATE_PIECES:], hcf + hcb, g_head[layer], g_sgu[layer], w_s[layer], b_s[layer],
                                   w_branch_a[layer], w_branch_b[layer], w_out[layer])
            hc = hc + mods_c[5][:, None, :] * y_ctx
            hc = ffn_sublayer(hc, mods_c[6], mods_c[7], mods_c[8], g_ffn2[layer], w_ffn2_in[layer], w_ffn2_out[layer])

        h = ffn_sublayer(h, mods[6], mods[7], mods[8], g_ffn2[layer], w_ffn2_in[layer], w_ffn2_out[layer])
    return rmsnorm(h, g_final)


def setup_inputs(seed=0):
    out = dict(first_inputs(seed))
    for name, value in second_inputs(seed + 1).items():
        if name != "x":
            out[name + "_2"] = value
    return out


def reference(
    x, a_w_qkv, a_w_o, a_lambda_q1, a_lambda_k1, a_lambda_q2, a_lambda_k2, a_subln_g, kv_norm_g,
    kv_w, b_w_q, b_w_o, mix_pre_g, mix_post_g, ffn_pre_g, ffn_post_g, ffn_w_gate_up, ffn_w_down,
    c_2, ctx_2, c_ctx_2, w_ada_2, b_ada_2, g_ffn1_2, w_ffn1_in_2, w_ffn1_out_2, g_mix_2, w_in_2,
    b_gates_2, conv_qk_w_2, conv_qk_b_2, g_head_2, g_sgu_2, w_s_2, b_s_2, w_branch_a_2,
    w_branch_b_2, w_out_2, g_ffn2_2, w_ffn2_in_2, w_ffn2_out_2, g_final_2,
):
    x = first_block(
        x, a_w_qkv, a_w_o, a_lambda_q1, a_lambda_k1, a_lambda_q2, a_lambda_k2, a_subln_g,
        kv_norm_g, kv_w, b_w_q, b_w_o, mix_pre_g, mix_post_g, ffn_pre_g, ffn_post_g,
        ffn_w_gate_up, ffn_w_down,
    )
    return second_block(
        x, c_2, ctx_2, c_ctx_2, w_ada_2, b_ada_2, g_ffn1_2, w_ffn1_in_2, w_ffn1_out_2, g_mix_2,
        w_in_2, b_gates_2, conv_qk_w_2, conv_qk_b_2, g_head_2, g_sgu_2, w_s_2, b_s_2,
        w_branch_a_2, w_branch_b_2, w_out_2, g_ffn2_2, w_ffn2_in_2, w_ffn2_out_2, g_final_2,
    )


_drawn_inputs = setup_inputs


def setup_inputs(seed=0):
    import zlib

    import numpy as np

    out = dict(_drawn_inputs(seed))
    spreads = {}
    factors = {'a_lambda_q2': 28.426,
     'a_subln_g': 2.877,
     'kv_norm_g': 15.724,
     'ffn_post_g': 3.616,
     'ctx_2': 8.0,
     'c_ctx_2': 5.57,
     'b_ada_2': 8.0,
     'g_ffn1_2': 8.0,
     'g_mix_2': 8.0,
     'b_gates_2': 2.862,
     'conv_qk_w_2': 64.0,
     'conv_qk_b_2': 64.0,
     'g_head_2': 64.0,
     'g_sgu_2': 8.0,
     'b_s_2': 8.0,
     'g_ffn2_2': 8.0}
    for name, (base, spread) in spreads.items():
        noise = np.random.default_rng([zlib.crc32(name.encode()), seed]).standard_normal(out[name].shape)
        drawn = base * np.exp(spread * noise) if base else spread * noise
        out[name] = __import__('jax').numpy.asarray(drawn.astype(out[name].dtype))
    for name, factor in factors.items():
        out[name] = (out[name] * factor).astype(out[name].dtype)
    return out
```

```python
import numpy as np
import concourse.bass as bass
from concourse import mybir
from contextlib import ExitStack

F32 = mybir.dt.float32
F32R = mybir.dt.float32r
ALU = mybir.AluOpType
ACT = mybir.ActivationFunctionType
AX = mybir.AxisListType.X

P = 128
D = 1024
T = 256
DFF = 2816
NF = DFF // P
NRAW = 4
NHL = 4
EPS = 1e-6

CC = {}
CW = 0
for _n, _w in [("id", 128), ("tle", 128), ("tge", 128), ("one", 128), ("mka", 384), ("rot", 128), ("cos", 256),
               ("sin", 256), ("mlt", 128), ("ngt", 128), ("neg", 128), ("mf", 128), ("mb", 128), ("sel", 2)]:
    CC[_n] = (CW, _w)
    CW += _w

VEC = {}
_r = 0
for _n, _k in [("kv_norm_g", 8), ("mix_pre_g", 16), ("ffn_pre_g", 16), ("g_ffn1_2", 8), ("g_mix_2", 8),
               ("g_ffn2_2", 8), ("g_head_2", 8), ("conv_qk_w_2", 48), ("a_subln_g", 1)]:
    VEC[_n] = (_r, _k)
    _r += _k
VEC["conv_qk_b_2"] = (128, 16)
VEC["c_2"] = (144, 8)
VEC["c_ctx_2"] = (152, 8)
NV2 = 32


def constants():
    c = np.zeros((P, CW), np.float32)

    def put(name, a):
        o, w = CC[name]
        c[:a.shape[0], o:o + w] = a

    i, j = np.arange(P)[:, None], np.arange(P)[None, :]
    put("id", (i == j).astype(np.float32))
    put("tle", (i <= j).astype(np.float32))
    put("tge", (i >= j).astype(np.float32))
    put("one", np.ones((P, P), np.float32))
    causal = np.where(j <= i, 0.0, -1e30).astype(np.float32)
    put("mka", np.concatenate([np.zeros((P, P), np.float32), causal, causal], 1))
    d = np.arange(P) % 64
    rot = np.zeros((P, P), np.float32)
    for m in range(P):
        if d[m] < 8:
            rot[m + 8, m] = -1.0
        elif d[m] < 16:
            rot[m - 8, m] = 1.0
    put("rot", rot)
    inv = (np.float32(500000.0) ** (-np.arange(0, 16, 2, dtype=np.float32) / np.float32(16))).astype(np.float32)
    ang = (np.arange(T, dtype=np.float32)[:, None] * inv[None, :]).astype(np.float32)
    cos, sin = np.cos(ang).T, np.sin(ang).T
    ct, st = np.ones((P, T), np.float32), np.zeros((P, T), np.float32)
    for m in range(P):
        if d[m] < 16:
            ct[m], st[m] = cos[d[m] % 8], sin[d[m] % 8]
    put("cos", ct)
    put("sin", st)
    put("mlt", (i < j).astype(np.float32))
    put("ngt", -(i >= j).astype(np.float32))
    put("neg", -np.ones((P, P), np.float32))
    put("mf", np.where(j <= i, 0.0, -1e30).astype(np.float32))
    put("mb", np.where(j >= i, 0.0, -1e30).astype(np.float32))
    sel = np.zeros((P, 2), np.float32)
    for g in range(4):
        sel[32 * g, 0] = 1.0
        sel[32 * g + 1, 1] = 1.0
    put("sel", sel)
    return c


def positions():
    t = np.arange(T)
    r, col = (t // 64).astype(np.float32), (t % 64).astype(np.float32)
    q = D // 4
    f = np.exp((-np.float32(np.log(10000.0)) * np.arange(q, dtype=np.float32) / np.float32(q)).astype(np.float32))
    ar, ac = (r[:, None] * f).astype(np.float32), (col[:, None] * f).astype(np.float32)
    return np.concatenate([np.sin(ar), np.cos(ar), np.sin(ac), np.cos(ac)], -1).astype(np.float32)


def program(nc, I, out):
    ctx = ExitStack()
    with ctx:
        base = (nc.sbuf_base + 63) // 64 * 64
        limit = nc.sbuf_usable_end

        cur = [base]

        def at(name, shape, off, dt=F32):
            n = 1
            for s in shape[1:]:
                n *= s
            assert off + 4 * n <= limit, (name, off + 4 * n - limit)
            return nc.alloc_sbuf_tensor_at(name, list(shape), dt, offset=off)

        def fixed(name, shape, dt=F32):
            n = 1
            for s in shape[1:]:
                n *= s
            t = at(name, shape, cur[0], dt)
            cur[0] += (4 * n + 31) // 32 * 32
            return t

        class Region:
            def __init__(self, start):
                self.o = start

            def __call__(self, name, shape, dt=F32):
                n = 1
                for s in shape[1:]:
                    n *= s
                t = at(name, shape, self.o, dt)
                self.o += (4 * n + 31) // 32 * 32
                return t

        RAW = [fixed(f"raw{i}", [P, 2048]) for i in range(NRAW)]
        WH = [fixed(f"wh{i}", [P, 1024], F32R) for i in range(NHL)]
        WL = [fixed(f"wl{i}", [P, 1024], F32R) for i in range(NHL)]
        X = fixed("X", [P, 2, D])
        XTH = fixed("XTH", [P, 8, T], F32R)
        XTL = fixed("XTL", [P, 8, T], F32R)
        C = fixed("C", [P, CW])
        CG = fixed("CG", [P, 128 + NV2])
        SM = fixed("SM", [P, 512])
        MODS = fixed("MODS", [P, 72, 2])
        AB = fixed("AB", [P, 40])
        G5 = fixed("G5", [P, D])
        G8 = fixed("G8", [P, D])
        TMP = [fixed(f"TMP{i}", [P, 512]) for i in range(4)]
        GB = [fixed(f"GB{i}", [P, D]) for i in range(1)]
        reg0 = cur[0]
        room = limit - reg0

        PS = [ctx.enter_context(nc.psum_tensor(f"ps{i}", [P, 512], F32)) for i in range(8)]

        sems = {e: ctx.enter_context(nc.semaphore(f"s_{e}")) for e in ("pe", "act", "dve", "pool")}
        for i in range(NRAW):
            sems[f"raw{i}"] = ctx.enter_context(nc.semaphore(f"s_raw{i}"))
        for n in ("cst", "vec", "x", "ctx", "gb", "lam", "bg", "wg", "pos", "ws", "bs", "sgu", "out"):
            sems[n] = ctx.enter_context(nc.semaphore(f"s_{n}"))

        Q, CNT, SEEN = {}, {}, {}

        def reset():
            for e in ("pe", "act", "dve", "pool", "sp"):
                Q[e] = []
                SEEN[e] = {}
            for s in sems:
                CNT[s] = 0

        def op(e, f, w=(), inc=1, sem=None):
            for s, v in w:
                if SEEN[e].get(s, 0) < v:
                    SEEN[e][s] = v
                    Q[e].append((None, sems[s], v))
            s = sem or e
            if inc:
                CNT[s] += inc
            Q[e].append((f, sems[s] if inc else None, inc))
            return (s, CNT[s])

        def dma(e, dst, src, sem, w=()):
            return op(e, lambda g: g.dma_start(dst, src), w, 16, sem)

        def mm(o, l, r, start, stop, w=(), inc=0, skip=False):
            return op("pe", lambda g: g.matmul(o, l, r, start=start, stop=stop, skip_group_check=skip), w, inc)

        def tr(o, i, w=(), inc=0):
            n = i.shape[0]
            return op("pe", lambda g: g.transpose(o, i, C[0:n, 0:n]), w, inc)

        def act(o, i, fn, w=(), bias=0.0, scale=1.0, acc=None):
            if acc is None:
                return op("act", lambda g: g.activation(o, i, fn, bias=bias, scale=scale), w)
            return op("act", lambda g: g.activation(o, i, fn, bias=bias, scale=scale, accum_out=acc), w)

        def tt(e, o, a, b, f, w=()):
            return op(e, lambda g: g.tensor_tensor(o, a, b, f), w)

        def ts(e, o, a, s1, s2, f1, f2=None, w=()):
            if f2 is None:
                return op(e, lambda g: g.tensor_scalar(o, a, s1, None, f1), w)
            return op(e, lambda g: g.tensor_scalar(o, a, s1, s2, f1, f2), w)

        def stt(o, a, s, b, f1, f2, w=()):
            return op("dve", lambda g: g.scalar_tensor_tensor(o, a, s, b, f1, f2), w)

        def sumsq(o, junk, a, w=()):
            return op("dve", lambda g: g.tensor_tensor_reduce(junk, a, a, 1.0, 0.0, ALU.mult, ALU.add, o), w)

        def cp(e, o, a, w=()):
            return op(e, lambda g: g.tensor_copy(o, a), w)

        def red(o, a, f, w=(), negate=False):
            if negate:
                return op("dve", lambda g: g.tensor_reduce(o, a, AX, f, negate=True), w)
            return op("dve", lambda g: g.tensor_reduce(o, a, AX, f), w)

        def recip(o, a, w=()):
            return op("dve", lambda g: g.reciprocal(o, a), w)

        def mset(e, o, v, w=()):
            return op(e, lambda g: g.memset(o, v), w)

        def con(name):
            o, w = CC[name]
            return C[:, o:o + w]

        def col(name, k=0):
            o, _ = VEC[name]
            return CG[:, o + k:o + k + 1]

        BANKS = []

        def take():
            return BANKS.pop(0)

        def give(b, t):
            BANKS.append((b, t))

        plan, ST = [], {}

        def stream_reset(known):
            ST.clear()
            ST.update(known=known, got=0, dma=0, split=0, sub=0, raw_free={}, hl_free={}, halves={}, landed={},
                      seq=[])

        def issue_dma(j):
            src, nk, nn, split = ST["known"][j]
            s = j % NRAW
            dst = RAW[s][:, 0:nk * nn].rearrange("p (k n) -> p k n", k=nk)
            ST["landed"][j] = dma("sp", dst, src, f"raw{s}", ST["raw_free"].get(j - NRAW, ()))

        def pump():
            while ST["dma"] < len(ST["known"]) and (ST["dma"] < NRAW or ST["dma"] - NRAW in ST["raw_free"]):
                issue_dma(ST["dma"])
                ST["dma"] += 1

        def split_chunk(j):
            src, nk, nn, split = ST["known"][j]
            raw = RAW[j % NRAW]
            halves, last = [], None
            n = nk * nn
            cuts = [(0, n // 2), (n // 2, n)] if n > 1024 else [(0, n)]
            for a, b in cuts:
                g = ST["sub"]
                s = g % NHL
                free = ST["hl_free"].get(g - NHL, ())
                h, l = WH[s][:, 0:b - a], WL[s][:, 0:b - a]
                t1 = act(h, raw[:, a:b], ACT.Copy, [ST["landed"][j], *free])
                t2 = tt("dve", l, raw[:, a:b], h.bitcast(F32), ALU.subtract, [t1, ST["landed"][j], *free])
                halves.append((h, l, t1, t2, g))
                ST["sub"] += 1
                last = t2
            ST["halves"][j] = halves
            ST["raw_free"][j] = [last]
            pump()

        def ahead(j):
            k = ST["split"]
            while k < len(ST["known"]) and k <= j:
                if ST["known"][k][3] and k not in ST["halves"]:
                    split_chunk(k)
                k += 1
            while k < len(ST["known"]) and not ST["known"][k][3]:
                k += 1
            ST["split"] = k

        def ahead_next():
            k = ST["split"]
            if k < len(ST["known"]) and k not in ST["halves"] and k in ST["landed"]:
                split_chunk(k)

        def get(src, nk, nn, split=True):
            j = ST["got"]
            ST["got"] += 1
            if ST["known"] is None:
                plan.append((src, nk, nn, split))
                return None
            assert ST["known"][j][1:] == (nk, nn, split)
            if split:
                ahead(j)
            return j

        def wsrc(wt, k0, nk, n0, nn):
            return wt[k0 * P:(k0 + nk) * P, n0:n0 + nn].rearrange("(k p) n -> p k n", p=P)

        def moving(wt, XH, XL, n0, kts, banks, w, k_first, k_last, ntt=2, nn=512, k_off=0):
            nk = len(kts)
            j = get(wsrc(wt, kts[0], nk, n0, nn), nk, nn)
            if j is None:
                return ("pe", 0)
            hv = ST["halves"][j]
            per = nk // len(hv)
            tok = None
            for i, (h, l, t1, t2, g) in enumerate(hv):
                hh, ll = h.rearrange("p (k n) -> p k n", k=per), l.rearrange("p (k n) -> p k n", k=per)
                for t in range(ntt):
                    for kk in range(per):
                        k = kts[i * per + kk]
                        a, b = XH[:, k - k_off, t * P:t * P + P], XL[:, k - k_off, t * P:t * P + P]
                        o = PS[banks[t]][:, 0:nn]
                        first = k == k_first
                        lastk = k == k_last
                        mm(o, a, hh[:, kk, :], first, False, [t1, *w])
                        mm(o, a, ll[:, kk, :], False, False, [t2])
                        end = (t == ntt - 1 and kk == per - 1)
                        tok = mm(o, b, hh[:, kk, :], False, lastk, (), 1 if (end or lastk) else 0)
                ST["hl_free"][g] = [tok]
            ahead_next()
            return tok

        def fixed_w(wt, XH, XL, n0, bank, w, tn=T):
            j = get(wsrc(wt, 0, 8, n0, 256), 8, 256)
            if j is None:
                return ("pe", 0)
            hv = ST["halves"][j]
            tok = None
            for f in range(2):
                o = PS[bank][:, f * T:f * T + tn]
                for i, (h, l, t1, t2, g) in enumerate(hv):
                    hh, ll = h.rearrange("p (k n) -> p k n", k=4), l.rearrange("p (k n) -> p k n", k=4)
                    for kk in range(4):
                        k = 4 * i + kk
                        a, b = hh[:, kk, f * P:f * P + P], ll[:, kk, f * P:f * P + P]
                        mm(o, a, XH[:, k, :], k == 0, False, [t1, *w])
                        mm(o, a, XL[:, k, :], False, False)
                        tok = mm(o, b, XH[:, k, :], False, k == 7, [t2], 1 if kk == 3 else 0)
                    if f == 1:
                        ST["hl_free"][g] = [tok]
            ahead_next()
            return tok

        smc = [0]

        def sm(n):
            if smc[0] + n > 512:
                smc[0] = 0
            a = SM[:, smc[0]:smc[0] + n]
            smc[0] += n
            return a

        def rstd(ss, n, count, w):
            v, l, y0, a, b, y = sm(n), sm(n), sm(n), sm(n), sm(n), sm(n)
            t = ts("dve", v, ss, 1.0 / count, EPS, ALU.mult, ALU.add, w)
            t = act(l, v, ACT.Ln, [t])
            t = act(y0, l, ACT.Exp, [t], scale=-0.5)
            t = tt("dve", a, y0, y0, ALU.mult, [t])
            t = tt("dve", b, a, v, ALU.mult, [t])
            t = ts("dve", a, b, -0.5, 1.5, ALU.mult, ALU.add, [t])
            t = tt("dve", y, y0, a, ALU.mult, [t])
            return y, t

        tmi = [0]
        TMF = {}

        def tmp():
            i = tmi[0] % 4
            tmi[0] += 1
            return i, TMP[i], TMF.get(i, [])

        def to_halves(src, nkt, H, L, scale, shift, w, wfree, k0=0):
            toks = []
            for k in range(0, nkt, 2):
                b, f = take()
                for kk in range(2):
                    for t in range(2):
                        tk = tr(PS[b][:, kk * T + t * P:kk * T + t * P + P], src(t, k + kk), [*w, *f],
                                1 if kk == 1 and t == 1 else 0)
                i, tm, fr = tmp()
                for kk in range(2):
                    t1 = act(tm[:, kk * T:kk * T + T], PS[b][:, kk * T:kk * T + T], ACT.Identity, [tk, *fr, *w],
                             bias=shift(k + kk), scale=scale(k + kk))
                give(b, [t1])
                tv = tm[:, :].rearrange("p (k t) -> p k t", k=2)
                h, l = H[:, k0 + k:k0 + k + 2, :], L[:, k0 + k:k0 + k + 2, :]
                t2 = cp("dve", h, tv, [t1, *wfree])
                t3 = tt("pool" if k % 4 == 0 else "dve", l, tv, h.bitcast(F32), ALU.subtract, [t1, t2, *wfree])
                TMF[i] = [t2, t3]
                toks += [t2, t3]
            return toks

        def norm_stats(x, w, junk0, junk1):
            ss = sm(2)
            t1 = act(junk0, x[:, 0, :], ACT.Square, w, acc=ss[:, 0:1])
            t2 = sumsq(ss[:, 1:2], junk1, x[:, 1, :], w)
            return rstd(ss, 2, D, [t1, t2])

        def normed(x, w, Y, wy):
            r, t = norm_stats(x, [*w, *wy], Y[:, 0, :], Y[:, 1, :])
            ta = ts("dve", Y[:, 0, :], x[:, 0, :], r[:, 0:1], None, ALU.mult, None, [t])
            tb = act(Y[:, 1, :], x[:, 1, :], ACT.Copy, [t], scale=r[:, 1:2])
            return [ta, tb]

        def evac_rows(Y, tile, n0, bank, tok, w, ss=None):
            t1 = act(Y[:, tile, n0:n0 + 512], PS[bank][:, :], ACT.Copy, [tok, *w])
            give(bank, [t1])
            if ss is None:
                return [t1]
            i, tm, fr = tmp()
            t2 = sumsq(ss, tm[:, :], Y[:, tile, n0:n0 + 512], [t1, *fr])
            TMF[i] = [t2]
            return [t1, t2]

        def rows_linear(wt, XH, XL, nk, w, done, ncols=D, n_base=0, k_off=0):
            for n0 in range(0, ncols, 512):
                (b0, f0), (b1, f1) = take(), take()
                k = 0
                tk = None
                while k < nk:
                    m = min(4, nk - k)
                    tk = moving(wt, XH, XL, n_base + n0, [k_off + z for z in range(k, k + m)], (b0, b1),
                                [*w, *f0, *f1], k_off, k_off + nk - 1, k_off=k_off)
                    k += m
                    if k < nk:
                        yield
                done(0, n0, b0, tk)
                done(1, n0, b1, tk)
                yield

        def load_gb(v, w):
            return dma("pool", GB[0][:, :], v.partition_broadcast(P) if len(v.shape) == 1 else v, "gb", w)

        def post_add(Y, ss, toks, gtok, x, wx):
            s2 = sm(2)
            t = tt("dve", s2, ss[:, 0:2], ss[:, 2:4], ALU.add, toks)
            r, t = rstd(s2, 2, D, [t])
            res = []
            for i in range(2):
                t1 = stt(Y[:, i, :], Y[:, i, :], r[:, i:i + 1], GB[0][:, :], ALU.mult, ALU.mult, [t, gtok, *toks])
                t2 = tt("dve", x[:, i, :], x[:, i, :], Y[:, i, :], ALU.add, [t1, *wx])
                res.append(t2)
            return res

        rF = Region(reg0)
        HTH = rF("HTH", [P, NF, T], F32R)
        HTL = rF("HTL", [P, NF, T], F32R)
        YF = rF("YF", [P, 2, D])
        XC = rF("XC", [P, 2, D])
        SG = [rF(f"SG{i}", [P, 512]) for i in range(2)]
        G2 = [rF(f"G2{i}", [P, D]) for i in range(2)]
        cT = rF("cT", [P, 8, 32])
        STG = rF("STG", [P, 512])
        BA = rF("BA", [18, 512])

        rA = Region(reg0)
        qT = rA("qT", [P, 8, T])
        kT = rA("kT", [P, 8, T])
        VA = rA("VA", [P, 2, D])
        OA = rA("OA", [P, 2, D])
        YA = rA("YA", [P, 2, D])
        SA = [rA(f"SA{i}", [P, 384]) for i in range(4)]
        PA = [rA(f"PA{i}", [P, 384]) for i in range(4)]
        TA = [rA(f"TA{i}", [P, 384]) for i in range(2)]
        LV = rA("LV", [P, 256])

        rB = Region(rA.o)
        VR = rB("VR", [P, 2, P])

        rM = Region(reg0)
        mqT = rM("mqT", [P, 8, T])
        mkT = rM("mkT", [P, 8, T])
        mk = rM("mk", [P, 2, D])
        mv = rM("mv", [P, 2, 4, 257])
        CS = rM("CS", [P, 2, 8, 257])
        Hm = rM("Hm", [P, 2, D])
        CVr = rM("CVr", [P, 2, 258])
        BG = rM("BG", [P, 16])
        WG = rM("WG", [P, 8, 16])
        GT = rM("GT", [P, 2, 16])
        LI = rM("LI", [P, 2, 8])
        LF = rM("LF", [P, 2, 8])
        GS = rM("GS", [P, 12, 16])
        rT = rM("rT", [8, T])
        VW = [rM(f"VW{i}", [P, 257]) for i in range(2)]
        DE = rM("DE", [P, 4, P])
        RM4 = rM("RM4", [P, 4, P])
        PPp = [rM(f"PP{i}", [P, P]) for i in range(2)]
        PPt = [rM(f"PT{i}", [P, P]) for i in range(2)]
        NUM = [rM(f"NUM{i}", [P, 257]) for i in range(2)]
        NX = rM("NX", [P, 257])
        MST = rM("MST", [P, 24])

        rG = Region(reg0)
        UU = rG("UU", [P, 2, D])
        VV = rG("VV", [P, 2, D])
        OO = rG("OO", [P, 2, D])
        GAA = rG("GAA", [P, 2, D])
        assert rG.o <= reg0 + 4 * 2048 * 4
        rG2 = Region(max(rM.o, rG.o))
        GBB = rG2("GBB", [P, 2, D])

        def build(known):
            reset()
            stream_reset(known)
            BANKS[:] = [(i, []) for i in range(8)]
            TMF.clear()
            tmi[0] = 0
            smc[0] = 0
            if known is not None:
                pump()

            tc = dma("act", C[:, :], I["cst"], "cst")
            tx = dma("act", X[:, :, :], I["x"][0].rearrange("(t p) d -> p t d", p=P), "x")
            tz = mset("pool", VR[:, :, :], 0.0)
            for n in VEC:
                o, k = VEC[n]
                s, o = o // 128, o % 128
                v = I[n]
                if len(v.shape) == 1:
                    src = v.rearrange("(a b) -> a b", b=P)
                elif len(v.shape) == 2:
                    src = v.rearrange("l (a b) -> (l a) b", b=P)
                else:
                    src = v.rearrange("l w (a b) -> (l w a) b", b=P)
                tv = dma("act", VR[o:o + k, s, :], src, "vec", [tz])
            b, f = take()
            tr(PS[b][:, 0:128], VR[:, 0, :], [tc, tv, *f])
            tk = tr(PS[b][:, 128:160], VR[0:NV2, 1, :], (), 1)
            tcg = act(CG[:, :], PS[b][:, 0:160], ACT.Copy, [tk])
            give(b, [tcg])
            for i, n in enumerate(["a_lambda_q1", "a_lambda_k1", "a_lambda_q2", "a_lambda_k2"]):
                tl = dma("act", LV[:, 64 * i:64 * i + 64], I[n][0].partition_broadcast(P), "lam")
            sl, el, lam = sm(2), sm(2), AB[:, 32:33]
            ta = op("dve", lambda g: g.tensor_tensor_reduce(TMP[0][:, 0:64], LV[:, 0:64], LV[:, 64:128], 1.0, 0.0,
                                                            ALU.mult, ALU.add, sl[:, 0:1]), [tl])
            tb = op("dve", lambda g: g.tensor_tensor_reduce(TMP[1][:, 0:64], LV[:, 128:192], LV[:, 192:256], 1.0,
                                                            0.0, ALU.mult, ALU.add, sl[:, 1:2]), [tl])
            ta = act(el, sl, ACT.Exp, [ta, tb])
            tlam = stt(lam, el[:, 1:2], -1.0, el[:, 0:1], ALU.mult, ALU.add, [ta])
            tlam = ts("dve", lam, lam, 0.8 - 0.6, None, ALU.add, None, [tlam])
            tsg = ts("dve", AB[:, 33:34], col("a_subln_g"), 1.0 - (0.8 - 0.6), None, ALU.mult, None, [tcg])
            for i in range(4):
                TMF[i] = [tlam]

            def gain(name, off=0):
                return lambda k: col(name, off + k)

            zero = lambda k: 0.0

            tn = normed(X, [tx], YA, [])
            th = to_halves(lambda t, k: YA[:, t, k * P:k * P + P], 8, XTH, XTL, gain("mix_pre_g"), zero,
                           [*tn, tcg], [])
            wq = I["a_w_qkv"][0]
            qk_done = []
            for i in range(8):
                b, f = take()
                tk = fixed_w(wq, XTH, XTL, 256 * i, b, [*th, *f])
                dst = (qT if i < 4 else kT)[:, 2 * (i % 4):2 * (i % 4) + 2, :].rearrange("p k t -> p (k t)")
                t1 = act(dst, PS[b][:, :], ACT.Copy, [tk])
                give(b, [t1])
                b, f = take()
                t2 = mm(PS[b][:, :], con("rot"), dst, True, True, [t1, tc, *f], 1)
                i_, tm, fr = tmp()
                v2 = lambda a: a.rearrange("p (k t) -> p k t", k=2)
                cosb = con("cos").unsqueeze(1).to_broadcast([P, 2, T])
                sinb = con("sin").unsqueeze(1).to_broadcast([P, 2, T])
                t3 = tt("dve", v2(tm[:, :]), v2(PS[b][:, :]), sinb, ALU.mult, [t2, tc, *fr])
                give(b, [t3])
                t4 = tt("pool", v2(dst), v2(dst), cosb, ALU.mult, [t2, t1, tc])
                t5 = tt("pool", dst, dst, tm[:, :], ALU.add, [t3, t4])
                TMF[i_] = [t5]
                qk_done.append(t5)

            v_done = []

            def dv(tile, n0, bank, tok):
                t1 = act(VA[:, tile, n0:n0 + 512], PS[bank][:, :], ACT.Copy, [tok])
                give(bank, [t1])
                v_done.append(t1)

            for _ in rows_linear(wq, XTH, XTL, 8, th, dv, n_base=2048):
                pass

            SAF, PAF, TAF = {}, {}, {}
            oss = sm(16)
            o_done = []
            tgb = load_gb(I["mix_post_g"][0], [])
            for h in range(8):
                bb = [take(), take()]
                sc = []
                for a in range(2):
                    b, f = bb[a]
                    q_, k_ = qT[64 * a:64 * a + 64, h, :], kT[64 * a:64 * a + 64, h, :]
                    mm(PS[b][:, 0:256], q_[:, 128:256], k_, True, True, [*qk_done, *f])
                    tk = mm(PS[b][:, 256:384], q_[:, 0:128], k_[:, 0:128], True, True, (), 1)
                    i = (2 * h + a) % 4
                    t1 = stt(SA[i][:, :], PS[b][:, 0:384], 0.125, con("mka"), ALU.mult, ALU.add,
                             [tk, *SAF.get(i, [])])
                    give(b, [t1])
                    nm, ls = sm(2), sm(2)
                    t2 = red(nm[:, 0:1], SA[i][:, 0:256], ALU.max, [t1], negate=True)
                    t3 = red(nm[:, 1:2], SA[i][:, 256:384], ALU.max, [t1], negate=True)
                    t4 = act(PA[i][:, 0:256], SA[i][:, 0:256], ACT.Exp, [t2, *PAF.get(i, [])], bias=nm[:, 0:1],
                             acc=ls[:, 0:1])
                    t5 = act(PA[i][:, 256:384], SA[i][:, 256:384], ACT.Exp, [t3], bias=nm[:, 1:2],
                             acc=ls[:, 1:2])
                    SAF[i] = [t4, t5]
                    rl = sm(2)
                    t6 = recip(rl, ls, [t4, t5])
                    if a == 1:
                        t6 = ts("dve", rl, rl, lam, None, ALU.mult, None, [t6, tlam])
                    sc.append((i, rl, [t4, t5, t6]))
                i0, r0, w0 = sc[0]
                i1, r1, w1 = sc[1]
                tks = []
                for c_, (lo, hi) in enumerate([(0, 256), (256, 384)]):
                    t7 = ts("dve", PA[i1][:, lo:hi], PA[i1][:, lo:hi], r1[:, c_:c_ + 1], None, ALU.mult, None, w1)
                    t8 = stt(PA[i0][:, lo:hi], PA[i0][:, lo:hi], r0[:, c_:c_ + 1], PA[i1][:, lo:hi], ALU.mult,
                             ALU.subtract, [*w0, t7])
                    tks.append(t8)
                PAF[i1] = tks
                b, f = take()
                tr(PS[b][:, 0:128], PA[i0][:, 256:384], [*tks, *f])
                tr(PS[b][:, 128:256], PA[i0][:, 0:128])
                tk = tr(PS[b][:, 256:384], PA[i0][:, 128:256], (), 1)
                PAF[i0] = [tk]
                t9 = act(TA[h % 2][:, :], PS[b][:, 0:384], ACT.Copy, [tk, *TAF.get(h % 2, [])])
                give(b, [t9])
                b, f = take()
                v0, v1 = VA[:, 0, h * P:h * P + P], VA[:, 1, h * P:h * P + P]
                mm(PS[b][:, 0:128], TA[h % 2][:, 0:128], v0, True, True, [t9, *v_done, *f])
                mm(PS[b][:, 128:256], TA[h % 2][:, 128:256], v0, True, False)
                tk = mm(PS[b][:, 128:256], TA[h % 2][:, 256:384], v1, False, True, (), 1)
                TAF[h % 2] = [tk]
                t1 = act(OA[:, :, h * P:h * P + P], PS[b][:, 0:256].rearrange("p (t d) -> p t d", t=2), ACT.Copy,
                         [tk])
                give(b, [t1])
                i_, tm, fr = tmp()
                for t in range(2):
                    t2 = sumsq(oss[:, 2 * h + t:2 * h + t + 1], tm[:, t * P:t * P + P], OA[:, t, h * P:h * P + P],
                               [t1, *fr])
                TMF[i_] = [t2]
                o_done += [t1, t2]
            r, t = rstd(oss, 16, 128, o_done)
            for h in range(8):
                for t_ in range(2):
                    o = OA[:, t_, h * P:h * P + P]
                    e = "pool" if t_ else "dve"
                    t1 = ts(e, o, o, r[:, 2 * h + t_:2 * h + t_ + 1], None, ALU.mult, None, [t])
                    o_done.append(t1)
            wfree = [o_done[0]]
            th = to_halves(lambda t, k: OA[:, t, k * P:k * P + P], 8, XTH, XTL, lambda k: AB[:, 33:34], zero,
                           [*o_done, tsg], [v_done[-1], tk])
            ss, res = sm(4), []

            def out_proj(Yb, ssb, resb, wY):
                def d_(tile, n0, bank, tok):
                    resb.extend(evac_rows(Yb, tile, n0, bank, tok, wY, ssb[:, tile + n0 // 256:tile + n0 // 256 + 1]))
                return d_

            for _ in rows_linear(I["a_w_o"][0], XTH, XTL, 8, th, out_proj(YA, ss, res, th)):
                pass
            xt = post_add(YA, ss, res, tgb, X, [])
            return_tok = xt
            def fence():
                return [(e, CNT[e]) for e in ("pe", "act", "dve", "pool")]

            SGF = {}

            def ffn(w_in, w_down, th, wreg, done):
                hs = []
                for c_ in range(11):
                    bg, fg = take()
                    tg = fixed_w(w_in, XTH, XTL, 256 * c_, bg, [*th, *fg])
                    i = c_ % 2
                    t1 = act(SG[i][:, :], PS[bg][:, :], ACT.Silu, [tg, *SGF.get(i, []), *wreg])
                    give(bg, [t1])
                    bu, fu = take()
                    tu = fixed_w(w_in, XTH, XTL, DFF + 256 * c_, bu, [*th, *fu])
                    i_, tm, fr = tmp()
                    t2 = tt("dve", tm[:, :], PS[bu][:, :], SG[i][:, :], ALU.mult, [t1, tu, *fr])
                    give(bu, [t2])
                    SGF[i] = [t2]
                    tv = tm[:, :].rearrange("p (k t) -> p k t", k=2)
                    h, l = HTH[:, 2 * c_:2 * c_ + 2, :], HTL[:, 2 * c_:2 * c_ + 2, :]
                    t3 = act(h, tv, ACT.Copy, [t2, *wreg])
                    t4 = tt("pool", l, tv, h.bitcast(F32), ALU.subtract, [t3, *wreg])
                    TMF[i_] = [t3, t4]
                    hs += [t3, t4]
                for _ in rows_linear(w_down, HTH, HTL, NF, hs, done):
                    pass
                return tu

            def block1_ffn(layer, x_tok):
                w0 = fence()
                tgb = load_gb(I["ffn_post_g"][layer], w0)
                tn = normed(X, x_tok, YF, w0)
                th = to_halves(lambda t, k: YF[:, t, k * P:k * P + P], 8, XTH, XTL, gain("ffn_pre_g", 8 * layer),
                               zero, tn, w0)
                ss, res = sm(4), []
                w1 = fence()
                ffn(I["ffn_w_gate_up"][layer], I["ffn_w_down"][layer], th, w0, out_proj(YF, ss, res, w1))
                return post_add(YF, ss, res, tgb, X, [])

            xt = block1_ffn(0, xt)

            w0 = fence()
            tgb = load_gb(I["mix_post_g"][1], w0)
            tn = normed(X, xt, YA, w0)
            th = to_halves(lambda t, k: YA[:, t, k * P:k * P + P], 8, XTH, XTL, gain("kv_norm_g"), zero, tn, w0)
            qk_done, v_done = [], []
            for i in range(4):
                b, f = take()
                tk = fixed_w(I["kv_w"], XTH, XTL, 256 * i, b, [*th, *f])
                dst = kT[:, 2 * i:2 * i + 2, :].rearrange("p k t -> p (k t)")
                t1 = act(dst, PS[b][:, :], ACT.Copy, [tk, *w0])
                give(b, [t1])
                qk_done.append(t1)
            for _ in rows_linear(I["kv_w"], XTH, XTL, 8, th, dv, n_base=1024):
                pass
            w1 = [v_done[-1], ("pe", CNT["pe"])]
            th = to_halves(lambda t, k: YA[:, t, k * P:k * P + P], 8, XTH, XTL, gain("mix_pre_g", 8), zero, tn, w1)
            for i in range(4):
                b, f = take()
                tk = fixed_w(I["b_w_q"][0], XTH, XTL, 256 * i, b, [*th, *f])
                dst = qT[:, 2 * i:2 * i + 2, :].rearrange("p k t -> p (k t)")
                t1 = act(dst, PS[b][:, :], ACT.Copy, [tk, *w0], scale=0.125)
                give(b, [t1])
                qk_done.append(t1)
            SAF.clear(); PAF.clear(); TAF.clear()
            o_done = []
            mlt = con("mlt")
            ob = None
            for hd in range(16):
                h, a = hd // 2, hd % 2
                q_, k_ = qT[64 * a:64 * a + 64, h, :], kT[64 * a:64 * a + 64, h, :]
                b, f = take()
                mm(PS[b][:, 0:256], k_[:, 0:128], q_, True, True, [*qk_done, *f])
                tk = mm(PS[b][:, 256:384], k_[:, 128:256], q_[:, 128:256], True, True, (), 1)
                i = hd % 4
                S_, P_ = SA[i], PA[i]
                t1 = act(S_[:, :], PS[b][:, 0:384], ACT.Abs, [tk, *SAF.get(i, [])])
                t2 = act(S_[:, :], S_[:, :], ACT.Exp, [t1], scale=-1.0)
                t3 = act(S_[:, :], S_[:, :], ACT.Ln, [t2], bias=1.0)
                t4 = stt(P_[:, :], PS[b][:, 0:384], 0.0, S_[:, :], ALU.max, ALU.add, [t3, *PAF.get(i, [])])
                t5 = tt("dve", P_[:, 0:128], P_[:, 0:128], mlt, ALU.mult, [t4])
                t6 = tt("dve", P_[:, 256:384], P_[:, 256:384], mlt, ALU.mult, [t4])
                o = PS[b]
                mm(o[:, 0:256], k_[:, 0:128], q_, True, False, [t4])
                mm(o[:, 0:256], con("ngt"), P_[:, 0:256], False, False, [t5, t6])
                mm(o[:, 128:256], con("neg"), P_[:, 256:384], False, True)
                mm(o[:, 256:384], k_[:, 128:256], q_[:, 128:256], True, False)
                tk = mm(o[:, 256:384], con("ngt"), P_[:, 256:384], False, True, (), 1)
                PAF[i] = [tk]
                t7 = act(S_[:, :], o[:, 0:384], ACT.Exp, [tk, t4])
                give(b, [t7])
                t8 = tt("pool", S_[:, 0:128], S_[:, 0:128], mlt, ALU.mult, [t7])
                t9 = tt("pool", S_[:, 256:384], S_[:, 256:384], mlt, ALU.mult, [t7])
                if hd % 4 == 0:
                    ob, of = take()
                v0, v1 = VA[:, 0, hd * 64:hd * 64 + 64], VA[:, 1, hd * 64:hd * 64 + 64]
                c0 = (hd % 4) * 64
                mm(PS[ob][:, c0:c0 + 64], S_[:, 0:128], v0, True, True, [t8, t9, *v_done, *of])
                mm(PS[ob][:, 256 + c0:256 + c0 + 64], S_[:, 128:256], v0, True, False)
                tk = mm(PS[ob][:, 256 + c0:256 + c0 + 64], S_[:, 256:384], v1, False, True, (), 1)
                SAF[i] = [tk]
                if hd % 4 == 3:
                    g4 = hd // 4
                    t1 = act(OA[:, :, g4 * 256:g4 * 256 + 256], PS[ob][:, :].rearrange("p (t d) -> p t d", t=2),
                             ACT.Copy, [tk])
                    give(ob, [t1])
                    o_done.append(t1)
            w1 = [("pe", CNT["pe"])]
            th = to_halves(lambda t, k: OA[:, t, k * P:k * P + P], 8, XTH, XTL, lambda k: 1.0, zero, o_done, w1)
            ss, res = sm(4), []
            for _ in rows_linear(I["b_w_o"][0], XTH, XTL, 8, th, out_proj(YA, ss, res, th)):
                pass
            xt = post_add(YA, ss, res, tgb, X, [])
            xt = block1_ffn(1, xt)

            w0 = fence()
            tctx = dma("pool", XC[:, :, :], I["ctx_2"][0].rearrange("(t p) d -> p t d", p=P), "ctx", w0)
            tba = dma("pool", BA[:, :], I["b_ada_2"].rearrange("l (a b) -> (l a) b", b=512), "bg", w0)
            tpos = dma("pool", YF[:, :, :], I["pos"].rearrange("(t p) d -> p t d", p=P), "pos", w0)
            tm0 = mset("pool", cT[:, :, :], 0.0, w0)
            tm1 = act(cT[:, :, 0], CG[:, 144:152], ACT.Silu, [tm0])
            tm1 = act(cT[:, :, 1], CG[:, 152:160], ACT.Silu, [tm1])
            xt = [tt("dve", X[:, i, :], X[:, i, :], YF[:, i, :], ALU.add, [tpos, *xt]) for i in range(2)]
            wa = I["w_ada_2"][0]
            stg_free = []
            mod_done = []
            for n in range(18):
                b, f = take()
                mm(PS[b][0:32, :], C[0:18, n:n + 1].to_broadcast([18, 32]), BA[:, :], True, False, [tba, *f], 0, True)
                for half in range(2):
                    j = get(wsrc(wa, 4 * half, 4, 512 * n, 512), 4, 512, False)
                    if j is None:
                        tk = ("pe", 0)
                        continue
                    raw = RAW[j % NRAW][:, :].rearrange("p (k n) -> p k n", k=4)
                    for kk in range(4):
                        tk = mm(PS[b][32 * kk:32 * kk + 32, :], cT[:, 4 * half + kk, :], raw[:, kk, :],
                                half == 0 and kk > 0, half == 1, [ST["landed"][j], tm1], 1 if kk == 3 else 0, True)
                    ST["raw_free"][j] = [tk]
                    pump()
                    ahead_next()
                t1 = cp("dve", STG[:, :], PS[b][:, :], [tk, *stg_free])
                give(b, [t1])
                v = n // 2
                b, f = take()
                if v in (2, 5, 8):
                    outs = {2: [(G2[0], 0), (G2[1], 1)], 5: [(G5, 0)], 8: [(G8, 0)]}[v]
                    fac = 1.0 if v == 5 else 0.5
                    stg_free = []
                    for qn, (gt, who) in enumerate(outs):
                        if qn:
                            b, f = take()
                        so = CC["sel"][0]
                        tk = mm(PS[b][:, :], C[:, so + who:so + who + 1].to_broadcast([P, P]), STG[:, :], True, True,
                                [t1, *f], 1)
                        t2 = act(gt[:, 512 * (n % 2):512 * (n % 2) + 512], PS[b][:, :], ACT.Copy, [tk, *w0],
                                 scale=fac)
                        give(b, [t2])
                        stg_free.append(tk)
                        mod_done.append(t2)
                else:
                    for z in range(4):
                        tk = mm(PS[b][:, 2 * z:2 * z + 2], STG[:, z * P:z * P + P], con("sel"), True, True, [t1, *f],
                                1 if z == 3 else 0)
                    t2 = cp("dve", MODS[:, 4 * n:4 * n + 4, :].rearrange("p a b -> p (a b)"), PS[b][:, 0:8], [tk])
                    give(b, [t2])
                    stg_free = [tk]
                    mod_done.append(t2)

            def modcols(name, v, who, w):
                t = stt(AB[:, 8 * who:8 * who + 8], MODS[:, 8 * (v + 1):8 * (v + 1) + 8, who], 1.0,
                        CG[:, VEC[name][0]:VEC[name][0] + 8], ALU.add, ALU.mult, [*mod_done, *w])
                return (lambda k: AB[:, 8 * who + k:8 * who + k + 1],
                        lambda k: MODS[:, 8 * v + k, who:who + 1], t)

            def gated(Y, G, x, xw, mult=True):
                res = []

                def d_(tile, n0, bank, tok):
                    i_, tm, fr = tmp()
                    t1 = tt("dve", tm[:, :], PS[bank][:, :], G[:, n0:n0 + 512], ALU.mult, [tok, *fr, *xw])
                    give(bank, [t1])
                    t2 = tt("pool", x[:, tile, n0:n0 + 512], x[:, tile, n0:n0 + 512], tm[:, :], ALU.add, [t1, *xw])
                    TMF[i_] = [t2]
                    res.append(t2)
                return d_, res

            def block2_ffn(name, w_in, w_out, v, who, G, x, xw):
                w0 = fence()
                sc, sh, t = modcols(name, v, who, w0)
                tn = normed(x, xw, YF, w0)
                th = to_halves(lambda t_, k: YF[:, t_, k * P:k * P + P], 8, XTH, XTL, sc, sh, [*tn, t], w0)
                d_, res = gated(None, G, x, w0)
                ffn(w_in, w_out, th, w0, d_)
                return res

            xct = block2_ffn("g_ffn1_2", I["w_ffn1_in_2"][0], I["w_ffn1_out_2"][0], 0, 1, G2[1], XC, [tctx])
            xt = block2_ffn("g_ffn1_2", I["w_ffn1_in_2"][0], I["w_ffn1_out_2"][0], 0, 0, G2[0], X, xt)

            w0 = fence()
            sc, sh, t = modcols("g_mix_2", 3, 1, w0)
            tn = normed(XC, xct, YF, w0)
            th_c = to_halves(lambda t_, k: YF[:, t_, k * P:k * P + P], 8, XTH, XTL, sc, sh, [*tn, t], w0)
            w1 = fence()
            win = I["w_in_2"][0]
            tbg = dma("pool", BG[:, :], I["b_gates_2"][0].partition_broadcast(P), "bg", w1)
            twg = dma("pool", WG[:, :, :], win[:, 3072:3088].rearrange("(k p) n -> p k n", p=P), "wg", w1)
            t1 = mset("pool", CVr[:, :, :], 0.0, w1)
            t2 = mset("pool", mv[:, :, :, 256:257], 1.0, w1)
            t3 = mset("pool", MST[:, :], 0.0, w1)
            ms_done = [t1, t2, t3]
            st = {"cv": [], "m": [t3], "cs": []}
            WGH = TMPW[0]
            WGL = TMPW[1]
            tw1 = cp("dve", WGH[:, :, :], WG[:, :, :], [twg, *w1])
            tw2 = tt("dve", WGL[:, :, :], WG[:, :, :], WGH[:, :, :].bitcast(F32), ALU.subtract, [tw1])

            def conv_feats(n0, base, dstT, scale, th, wdst, kc=None):
                res = []
                for i in range(4):
                    b, f = take()
                    tk = fixed_w(win, XTH, XTL, n0 + 256 * i, b, [*th, *f])
                    t1 = act(CVr[:, :, 1:257], PS[b][:, :].rearrange("p (k t) -> p k t", k=2), ACT.Copy,
                             [tk, *st["cv"], *ms_done])
                    give(b, [t1])
                    i_, tm, fr = tmp()
                    rd = []
                    for f2 in range(2):
                        ft = base + 2 * i + f2
                        o = tm[:, f2 * T:f2 * T + T]
                        ta = ts("dve", o, CVr[:, f2, 0:256], col("conv_qk_w_2", ft), col("conv_qk_b_2", ft),
                                ALU.mult, ALU.add, [t1, *fr])
                        ta = stt(o, CVr[:, f2, 1:257], col("conv_qk_w_2", 16 + ft), o, ALU.mult, ALU.add, [ta])
                        ta = stt(o, CVr[:, f2, 2:258], col("conv_qk_w_2", 32 + ft), o, ALU.mult, ALU.add, [ta])
                        rd.append(ta)
                    st["cv"] = rd
                    dst = dstT[:, 2 * i:2 * i + 2, :].rearrange("p k t -> p (k t)")
                    t3 = act(dst, tm[:, :], ACT.Silu, [*rd, *wdst])
                    TMF[i_] = [t3]
                    if scale != 1.0:
                        t3 = ts("pool", dst, dst, scale, None, ALU.mult, None, [t3])
                    res.append(t3)
                    if kc is not None:
                        b, f = take()
                        for f2 in range(2):
                            for t_ in range(2):
                                tk = tr(PS[b][:, t_ * 256 + f2 * P:t_ * 256 + f2 * P + P],
                                        dstT[:, 2 * i + f2, t_ * P:t_ * P + P], [t3, *f],
                                        1 if f2 == 1 and t_ == 1 else 0)
                        t4 = act(kc[:, :, 256 * i:256 * i + 256], PS[b][:, :].rearrange("p (t d) -> p t d", t=2),
                                 ACT.Copy, [tk, *wdst])
                        give(b, [t4])
                        res.append(t4)
                return res

            def values(th, wdst):
                res = []

                def d_(tile, n0, bank, tok):
                    t1 = act(mv[:, tile, n0 // 256:n0 // 256 + 2, 0:256],
                             PS[bank][:, :].rearrange("p (h d) -> p h d", h=2), ACT.Copy, [tok, *wdst])
                    give(bank, [t1])
                    res.append(t1)
                for _ in rows_linear(win, XTH, XTL, 8, th, d_, n_base=2048):
                    pass
                return res

            def gates(th, w):
                b, f = take()
                for t_ in range(2):
                    for k in range(8):
                        a, l = XTH[:, k, t_ * P:t_ * P + P], XTL[:, k, t_ * P:t_ * P + P]
                        o = PS[b][:, 16 * t_:16 * t_ + 16]
                        mm(o, a, WGH[:, k, :], k == 0, False, [*th, tw1, tw2, *f])
                        mm(o, a, WGL[:, k, :], False, False)
                        tk = mm(o, l, WGH[:, k, :], False, k == 7, (), 1 if k == 7 else 0)
                t1 = tt("dve", GT[:, :, :], PS[b][:, 0:32].rearrange("p (t c) -> p t c", t=2),
                        BG[:, :].unsqueeze(1).to_broadcast([P, 2, 16]), ALU.add, [tk, tbg, *w])
                give(b, [t1])
                g4 = GT[:, :, :].rearrange("p t (d z h) -> p t d z h", d=2, z=2)
                li = LI[:, :, :].rearrange("p t (d h) -> p t d h", d=2)
                lf = LF[:, :, :].rearrange("p t (d h) -> p t d h", d=2)
                s1 = GS[:, 0, :].rearrange("p (t d h) -> p t d h", t=2, d=2)
                t2 = cp("dve", li, g4[:, :, :, 0, :], [t1])
                t3 = cp("dve", lf, g4[:, :, :, 1, :], [t1])
                f16 = LF[:, :, :].rearrange("p t c -> p (t c)")
                t4 = act(GS[:, 0, :], f16, ACT.Abs, [t3])
                t4 = act(GS[:, 0, :], GS[:, 0, :], ACT.Exp, [t4], scale=-1.0)
                t4 = act(GS[:, 0, :], GS[:, 0, :], ACT.Ln, [t4], bias=1.0)
                t5 = stt(f16, f16, 0.0, GS[:, 0, :], ALU.min, ALU.subtract, [t4])
                b, f = take()
                z = PS[b]
                for t_ in range(2):
                    mm(z[:, 8 * t_:8 * t_ + 4], con("tle"), LF[:, t_, 0:4], True, True, [t5, *f])
                    mm(z[:, 8 * t_ + 4:8 * t_ + 8], con("tge"), LF[:, t_, 4:8], True, True)
                    tk = mm(z[:, 16 + 8 * t_:24 + 8 * t_], con("one"), LF[:, t_, :], True, True, (), 1)
                t6 = cp("dve", GS[:, 1:3, :].rearrange("p a b -> p (a b)"), z[:, 0:32], [tk])
                give(b, [t6])
                t7 = tt("dve", GS[:, 3, :], LI[:, :, :].rearrange("p t c -> p (t c)"), GS[:, 1, :], ALU.subtract,
                        [t6, t2])
                b, f = take()
                for t_ in range(2):
                    tk = tr(PS[b][0:8, t_ * P:t_ * P + P], GS[:, 3, 8 * t_:8 * t_ + 8], [t7, *f], 1)
                t8 = cp("dve", rT[:, :], PS[b][0:8, 0:256], [tk])
                give(b, [t8])
                t9 = red(GS[0:8, 4, 0:2], rT[:, :].rearrange("p (t s) -> p t s", t=2), ALU.max, [t8])
                for t_ in range(2):
                    t9 = ts("dve", GS[0:8, 5, 8 * t_:8 * t_ + 8], C[0:8, 0:8], GS[0:8, 4, t_:t_ + 1], None,
                            ALU.mult, None, [t9, tc])
                b, f = take()
                tk = mm(PS[b][:, 0:16], C[0:8, CC["one"][0]:CC["one"][0] + P], GS[0:8, 5, :], True, True, [t9, *f],
                        1)
                t10 = cp("dve", GS[:, 6, :], PS[b][:, 0:16], [tk])
                give(b, [t10])
                return [t7, t8, t10, t6]

            VWF = {}

            def mx_step(d, t_, w):
                s = slice(8 * t_ + 4 * d, 8 * t_ + 4 * d + 4)
                m, mxx = MST[:, 4 * d:4 * d + 4], MST[:, 8 + 4 * d:12 + 4 * d]
                t = tt("dve", mxx, m, GS[:, 6, s], ALU.max, w)
                ta = tt("dve", GS[:, 7, s], m, mxx, ALU.subtract, [t])
                tb = tt("dve", GS[:, 8, s], GS[:, 3, s], mxx, ALU.subtract, [t])
                tn_ = tt("dve", m, GS[:, 2, s], mxx, ALU.add, [t, ta])
                ta = act(GS[:, 7, s], GS[:, 7, s], ACT.Exp, [ta])
                tb = act(GS[:, 8, s], GS[:, 8, s], ACT.Exp, [tb])
                return [ta, tb, tn_]

            vwi = [0]

            def update(d, t_, w, first):
                res = []
                for h in range(4):
                    c = 8 * t_ + 4 * d + h
                    i = vwi[0] % 2
                    vwi[0] += 1
                    t1 = act(VW[i][:, :], mv[:, t_, h, :], ACT.Copy, [*w, *VWF.get(i, [])], scale=GS[:, 8, c:c + 1])
                    for z in range(2):
                        b, f = take()
                        tk = mm(PS[b][:, 0:257], mk[:, t_, h * 256 + z * P:h * 256 + z * P + P], VW[i][:, :], True,
                                True, [t1, *w, *f], 1)
                        dst = CS[:, z, 4 * d + h, :]
                        if first:
                            t2 = cp("dve", dst, PS[b][:, 0:257], [tk, *w])
                        else:
                            t2 = stt(dst, dst, GS[:, 7, c:c + 1], PS[b][:, 0:257], ALU.mult, ALU.add, [tk, *w])
                        give(b, [t2])
                        res.append(t2)
                    VWF[i] = [tk]
                return res

            kw = conv_feats(1024, 8, mkT, 1.0, th_c, w1, mk)
            vw = values(th_c, w1)
            gw = gates(th_c, w1)
            su = [*kw, *vw, *gw]
            for s_ in range(2):
                a = []
                for d in range(2):
                    t_ = s_ if d == 0 else 1 - s_
                    a.append((d, t_, mx_step(d, t_, su)))
                nx = []
                for d, t_, w in a:
                    nx += update(d, t_, [*su, *w], s_ == 0)
                su = su + nx

            w0 = fence()
            sc, sh, t = modcols("g_mix_2", 3, 0, w0)
            tn = normed(X, xt, Hm, w0)
            th = to_halves(lambda t_, k: Hm[:, t_, k * P:k * P + P], 8, XTH, XTL, sc, sh, [*tn, t], w0)
            gw = gates(th, w0)
            qw = conv_feats(0, 0, mqT, 0.0625, th, w0)
            kw = conv_feats(1024, 8, mkT, 1.0, th, w0, mk)
            vw = values(th, w0)
            w0 = fence()
            lw = [*gw, *qw, *kw, *vw]
            h_done = []
            PPF = {}
            ui = 0
            for s_ in range(2):
                for d in range(2):
                    t_ = s_ if d == 0 else 1 - s_
                    sl_ = slice(8 * t_ + 4 * d, 8 * t_ + 4 * d + 4)
                    m = MST[:, 4 * d:4 * d + 4]
                    b, f = take()
                    for h in range(4):
                        j = 4 * d + h
                        tk = mm(PS[b][:, h * P:h * P + P], C[0:8, j:j + 1].to_broadcast([8, P]),
                                rT[:, t_ * P:t_ * P + P], True, True, [*lw, *f], 1 if h == 3 else 0)
                    msk = con("mf" if d == 0 else "mb").unsqueeze(1).to_broadcast([P, 4, P])
                    t1 = tt("dve", RM4[:, :, :], PS[b][:, :].rearrange("p (h s) -> p h s", h=4), msk, ALU.add,
                            [tk, *h_done])
                    give(b, [t1])
                    M = MST[:, 16:20]
                    t2 = red(M, RM4[:, :, :], ALU.max, [t1])
                    t3 = tt("dve", M, M, m, ALU.max, [t2])
                    t4 = tt("dve", GS[:, 9, 0:4], m, M, ALU.subtract, [t3])
                    t5 = stt(GS[:, 9, 4:8], GS[:, 1, sl_], -1.0, M, ALU.mult, ALU.subtract, [t3])
                    t6 = ts("dve", GS[:, 9, 8:12], M, -1.0, None, ALU.mult, None, [t3])
                    t7 = act(GS[:, 10, 0:8], GS[:, 9, 0:8], ACT.Exp, [t4, t5, *h_done])
                    tD = []
                    for h in range(4):
                        tD.append(act(DE[:, h, :], RM4[:, h, :], ACT.Exp, [t6, t1, *h_done],
                                      bias=GS[:, 9, 8 + h:9 + h]))
                    new = []
                    for h in range(4):
                        i = ui % 2
                        ui += 1
                        b, f = take()
                        for z in range(2):
                            tk = mm(PS[b][:, 0:P], mqT[:, 2 * h + z, t_ * P:t_ * P + P],
                                    mkT[:, 2 * h + z, t_ * P:t_ * P + P], z == 0, z == 1, [*lw, *f], 1 if z else 0)
                        t8 = tt("dve", PPp[i][:, :], PS[b][:, 0:P], DE[:, h, :], ALU.mult,
                                [tk, tD[h], *PPF.get(i, [])])
                        give(b, [t8])
                        b, f = take()
                        tk = tr(PS[b][:, 0:P], PPp[i][:, :], [t8, *f], 1)
                        t9 = act(PPt[i][:, :], PS[b][:, 0:P], ACT.Copy, [tk, *PPF.get(i, [])])
                        give(b, [t9])
                        b, f = take()
                        tn1 = mm(PS[b][:, 0:257], PPt[i][:, :], mv[:, t_, h, :], True, True, [t9, *f], 1)
                        b2, f2 = take()
                        for z in range(2):
                            tn2 = mm(PS[b2][:, 0:257], mqT[:, 2 * h + z, t_ * P:t_ * P + P],
                                     CS[:, z, 4 * d + h, :], z == 0, z == 1, [*su, *f2], 1 if z else 0)
                        ta = act(NX[:, :], PS[b2][:, 0:257], ACT.Copy, [tn2, t7, *PPF.get("nx", [])],
                                 scale=GS[:, 10, h:h + 1])
                        give(b2, [ta])
                        tb = tt("dve", NUM[i][:, :], PS[b][:, 0:257], NX[:, :], ALU.add, [tn1, ta])
                        give(b, [tb])
                        PPF["nx"] = [tb]
                        PPF[i] = [tn1]
                        dn, rc = sm(1), sm(1)
                        tb2 = stt(dn, NUM[i][:, 256:257], -1.0, NUM[i][:, 256:257], ALU.mult, ALU.max, [tb])
                        tb2 = tt("dve", dn, dn, GS[:, 10, 4 + h:5 + h], ALU.max, [tb2, t7])
                        tb2 = recip(rc, dn, [tb2])
                        ho = Hm[:, t_, 256 * h:256 * h + 256]
                        if s_ == 0:
                            tc2 = ts("dve", ho, NUM[i][:, 0:256], rc, None, ALU.mult, None, [tb2, *w0])
                        else:
                            tc2 = stt(ho, NUM[i][:, 0:256], rc, ho, ALU.mult, ALU.add, [tb2])
                        new.append(tc2)
                    h_done = [*tD, t7, *new]
                    if s_ == 0:
                        w_ = mx_step(d, t_, [*h_done, *lw])
                        su = su + update(d, t_, [*h_done, *w_, *lw, ("pe", CNT["pe"])], False) + w_

            bst, bag, var = MSTAT[0], MSTAT[1], MSTAT[2]
            tks = []
            for t_ in range(2):
                for h in range(4):
                    i = 4 * t_ + h
                    o1, o2, src = bst[:, 6 * i:6 * i + 6], bag[:, 2 * i:2 * i + 2], Hm[:, t_, 256 * h:256 * h + 256]
                    t1 = op("dve", lambda g, o1=o1, src=src: g.bn_stats(o1, src), h_done)
                    t2 = op("dve", lambda g, o1=o1, o2=o2: g.bn_aggr(o2, o1), [t1])
                    tks.append(t2)
            bv = bag[:, 0:16].rearrange("p (i z) -> p i z", z=2)
            r, t = rstd(bv[:, :, 1], 8, 1, tks)
            for t_ in range(2):
                for h in range(4):
                    i = 4 * t_ + h
                    o = Hm[:, t_, 256 * h:256 * h + 256]
                    tks.append(ts("dve", o, o, bag[:, 2 * i:2 * i + 1], r[:, i:i + 1], ALU.subtract, ALU.mult, [t]))

            w0 = fence()
            tgb = load_gb(I["g_sgu_2"][0], w0)
            tws = dma("pool", WS[:, :, :], I["w_s_2"][0].rearrange("g t s -> t g s"), "ws", w0)
            tbs = dma("pool", BSR[:, :], I["b_s_2"][0], "bs", w0)

            def plain(dst, n_base, fn):
                res = []

                def d_(tile, n0, bank, tok):
                    t1 = act(dst[:, tile, n0:n0 + 512], PS[bank][:, :], fn, [tok, *w0])
                    give(bank, [t1])
                    res.append(t1)
                for _ in rows_linear(win, XTH, XTL, 8, th, d_, n_base=n_base):
                    pass
                return res

            tvs = plain(VV, 5136, ACT.Gelu_apprx_tanh)
            tuu = plain(UU, 4112, ACT.Gelu_apprx_tanh)
            too = plain(OO, 3088, ACT.Sigmoid)
            tga = plain(GAA, 6160, ACT.Sigmoid)
            tgbb = plain(GBB, 7184, ACT.Sigmoid)
            b, f = take()
            for g_ in range(4):
                tk = tr(PS[b][:, g_ * P:g_ * P + P], WS[:, g_, :], [tws, *f], 1 if g_ == 3 else 0)
            t1 = act(WST[:, :, :].rearrange("p g t -> p (g t)"), PS[b][:, :], ACT.Copy, [tk, *w0])
            give(b, [t1])
            b, f = take()
            tk = tr(PS[b][:, 0:4], BSR[:, :], [tbs, *f], 1)
            t2 = cp("dve", BSC[:, :], PS[b][:, 0:4], [tk, *w0])
            give(b, [t2])
            ss = sm(2)
            ssq = sm(4)
            t3s = []
            for t_ in range(2):
                for hf in range(2):
                    i_, tm, fr = tmp()
                    t3 = sumsq(ssq[:, 2 * hf + t_:2 * hf + t_ + 1], tm[:, :], VV[:, t_, 512 * hf:512 * hf + 512],
                               [*tvs, *fr])
                    TMF[i_] = [t3]
                    t3s.append(t3)
            t3 = tt("dve", ss, ssq[:, 0:2], ssq[:, 2:4], ALU.add, t3s)
            r, t = rstd(ss, 2, D, [t3])
            vn = [stt(VV[:, t_, :], VV[:, t_, :], r[:, t_:t_ + 1], GB[0][:, :], ALU.mult, ALU.mult, [t, tgb])
                  for t_ in range(2)]
            yb = []
            for t_ in range(2):
                for g2 in range(2):
                    b, f = take()
                    for gg in range(2):
                        g_ = 2 * g2 + gg
                        tk = mm(PS[b][:, gg * 256:gg * 256 + 256], WST[:, g_, :], VV[:, t_, g_ * 256:g_ * 256 + 256],
                                True, True, [t1, *vn, *f], 1 if gg else 0)
                    for gg in range(2):
                        g_ = 2 * g2 + gg
                        uo = UU[:, t_, g_ * 256:g_ * 256 + 256]
                        t4 = stt(uo, PS[b][:, gg * 256:gg * 256 + 256], BSC[:, g_:g_ + 1], uo, ALU.add, ALU.mult,
                                 [tk, t2, *tuu])
                        yb.append(t4)
                    give(b, [t4])
            ya = [tt("dve" if t_ else "pool", Hm[:, t_, :], Hm[:, t_, :], OO[:, t_, :], ALU.mult, [*too, *tks])
                  for t_ in range(2)]
            w1 = fence()
            th = to_halves(lambda t_, k: Hm[:, t_, k * P:k * P + P], 8, XTH, XTL, gain("g_head_2"), zero, ya, w1)
            res = []

            def da(tile, n0, bank, tok):
                g_ = GAA[:, tile, n0:n0 + 512]
                t1 = tt("dve", g_, PS[bank][:, :], g_, ALU.mult, [tok, *tga])
                give(bank, [t1])
                res.append(t1)

            for _ in rows_linear(I["w_branch_a_2"][0], XTH, XTL, 8, th, da):
                pass
            w1 = fence()
            th = to_halves(lambda t_, k: UU[:, t_, k * P:k * P + P], 8, XTH, XTL, lambda k: 1.0, zero, yb, w1)

            def db(tile, n0, bank, tok):
                g_ = GBB[:, tile, n0:n0 + 512]
                t1 = tt("dve", g_, PS[bank][:, :], g_, ALU.mult, [tok, *tgbb])
                give(bank, [t1])
                t2 = tt("pool", g_, g_, GAA[:, tile, n0:n0 + 512], ALU.add, [t1, *res])
                res2.append(t2)

            res2 = []
            for _ in rows_linear(I["w_branch_b_2"][0], XTH, XTL, 8, th, db):
                pass
            w1 = fence()
            th = to_halves(lambda t_, k: GBB[:, t_, k * P:k * P + P], 8, XTH, XTL, lambda k: 1.0, zero, res2, w1)
            d_, res = gated(None, G5, X, fence())
            for _ in rows_linear(I["w_out_2"][0], XTH, XTL, 8, th, d_):
                pass
            xt = block2_ffn("g_ffn2_2", I["w_ffn2_in_2"][0], I["w_ffn2_out_2"][0], 6, 0, G8, X, res)
            w0 = fence()
            tgb = load_gb(I["g_final_2"], w0)
            r, t = norm_stats(X, xt + w0, YF[:, 0, :], YF[:, 1, :])
            for t_ in range(2):
                t1 = stt(YF[:, t_, :], X[:, t_, :], r[:, t_:t_ + 1], GB[0][:, :], ALU.mult, ALU.mult, [t, tgb])
                to = dma("sp", out[0, t_ * P:t_ * P + P, :], YF[:, t_, :], "out", [t1])
            Q["sp"].append((None, sems["out"], to[1]))

        TMPW = [rM(f"WG{n}", [P, 8, 16], F32R) for n in "HL"]
        MSTAT = [rM("bst", [P, 48]), rM("bag", [P, 16]), None]
        WS = rG2("WS", [P, 4, P])
        WST = rG2("WST", [P, 4, P])
        BSR = rG2("BSR", [4, P])
        BSC = rG2("BSC", [P, 4])

        build(None)
        known = list(plan)
        build(known)

        block = ctx.enter_context(nc.Block())

        def play(eng, items):
            for f, s, v in items:
                if f is None:
                    eng.wait_ge(s, v)
                else:
                    i = f(eng)
                    if s is not None:
                        i.then_inc(s, v)

        @block.sync
        def _(eng):
            play(eng, Q["sp"])

        @block.tensor
        def _(eng):
            play(eng, Q["pe"])

        @block.scalar
        def _(eng):
            play(eng, Q["act"])

        @block.vector
        def _(eng):
            play(eng, Q["dve"])

        @block.gpsimd
        def _(eng):
            play(eng, Q["pool"])


_INS = [
    "x", "a_w_qkv", "a_w_o", "a_lambda_q1", "a_lambda_k1", "a_lambda_q2", "a_lambda_k2", "a_subln_g", "kv_norm_g",
    "kv_w", "b_w_q", "b_w_o", "mix_pre_g", "mix_post_g", "ffn_pre_g", "ffn_post_g", "ffn_w_gate_up", "ffn_w_down",
    "c_2", "ctx_2", "c_ctx_2", "w_ada_2", "b_ada_2", "g_ffn1_2", "w_ffn1_in_2", "w_ffn1_out_2", "g_mix_2", "w_in_2",
    "b_gates_2", "conv_qk_w_2", "conv_qk_b_2", "g_head_2", "g_sgu_2", "w_s_2", "b_s_2", "w_branch_a_2",
    "w_branch_b_2", "w_out_2", "g_ffn2_2", "w_ffn2_in_2", "w_ffn2_out_2", "g_final_2",
]


def kernel(**inputs):
    import numpy as _np
    import concourse.bacc as _bacc
    from concourse import mybir as _mybir
    from concourse.bass_utils import run_bass_kernel_spmd as _run

    nc = _bacc.Bacc("TRN2", target_bir_lowering=False, num_devices=1)
    arrays, args = {}, {}
    for name in _INS:
        arrays[name] = _np.ascontiguousarray(inputs[name])
    arrays["cst"] = constants()
    arrays["pos"] = positions()
    ins = {}
    for name, a in arrays.items():
        ins[f"in_{name}_dram"] = a
        args[name] = nc.dram_tensor(f"in_{name}_dram", a.shape, _mybir.dt.from_np(a.dtype), kind="ExternalInput").ap()
    out = nc.dram_tensor("out_0_dram", (1, 256, 1024), _mybir.dt.float32, kind="ExternalOutput").ap()
    program(nc, args, out)
    r = _run(nc, [ins], core_ids=[0])
    return r.results[0]["out_0_dram"]
```

```python
import numpy as np
import concourse.bass as bass
from concourse import mybir
from contextlib import ExitStack

F32 = mybir.dt.float32
F32R = mybir.dt.float32r
ALU = mybir.AluOpType
ACT = mybir.ActivationFunctionType
AX = mybir.AxisListType.X

P = 128
D = 1024
T = 256
DFF = 2816
NF = DFF // P
NRAW = 4
NHL = 4
EPS = 1e-6

CC = {}
CW = 0
for _n, _w in [("id", 128), ("tle", 128), ("tge", 128), ("one", 128), ("mka", 384), ("rot", 128), ("mlt", 128),
               ("ngt", 128), ("neg", 128), ("mb", 128), ("sel", 2), ("cos", 256), ("sin", 256)]:
    CC[_n] = (CW, _w)
    CW += _w

CK = CC["cos"][0]

VEC = {}
_r = 0
for _n, _k in [("kv_norm_g", 8), ("mix_pre_g", 16), ("ffn_pre_g", 16), ("g_ffn1_2", 8), ("g_mix_2", 8),
               ("g_ffn2_2", 8), ("g_head_2", 8), ("conv_qk_w_2", 48), ("a_subln_g", 1)]:
    VEC[_n] = (_r, _k)
    _r += _k
VEC["conv_qk_b_2"] = (128, 16)
VEC["c_2"] = (144, 8)
VEC["c_ctx_2"] = (152, 8)
NV2 = 32


def constants():
    c = np.zeros((P, CW), np.float32)

    def put(name, a):
        o, w = CC[name]
        c[:a.shape[0], o:o + w] = a

    i, j = np.arange(P)[:, None], np.arange(P)[None, :]
    put("id", (i == j).astype(np.float32))
    put("tle", (i <= j).astype(np.float32))
    put("tge", (i >= j).astype(np.float32))
    put("one", np.ones((P, P), np.float32))
    causal = np.where(j <= i, 0.0, -1e30).astype(np.float32)
    put("mka", np.concatenate([np.zeros((P, P), np.float32), causal, causal], 1))
    d = np.arange(P) % 64
    rot = np.zeros((P, P), np.float32)
    for m in range(P):
        if d[m] < 8:
            rot[m + 8, m] = -1.0
        elif d[m] < 16:
            rot[m - 8, m] = 1.0
    put("rot", rot)
    inv = (np.float32(500000.0) ** (-np.arange(0, 16, 2, dtype=np.float32) / np.float32(16))).astype(np.float32)
    ang = (np.arange(T, dtype=np.float32)[:, None] * inv[None, :]).astype(np.float32)
    cos, sin = np.cos(ang).T, np.sin(ang).T
    ct, st = np.ones((P, T), np.float32), np.zeros((P, T), np.float32)
    for m in range(P):
        if d[m] < 16:
            ct[m], st[m] = cos[d[m] % 8], sin[d[m] % 8]
    put("cos", ct)
    put("sin", st)
    put("mlt", (i < j).astype(np.float32))
    put("ngt", -(i >= j).astype(np.float32))
    put("neg", -np.ones((P, P), np.float32))
    put("mb", np.where(j >= i, 0.0, -1e30).astype(np.float32))
    sel = np.zeros((P, 2), np.float32)
    for g in range(4):
        sel[32 * g, 0] = 1.0
        sel[32 * g + 1, 1] = 1.0
    put("sel", sel)
    return c


def positions():
    t = np.arange(T)
    r, col = (t // 64).astype(np.float32), (t % 64).astype(np.float32)
    q = D // 4
    f = np.exp((-np.float32(np.log(10000.0)) * np.arange(q, dtype=np.float32) / np.float32(q)).astype(np.float32))
    ar, ac = (r[:, None] * f).astype(np.float32), (col[:, None] * f).astype(np.float32)
    return np.concatenate([np.sin(ar), np.cos(ar), np.sin(ac), np.cos(ac)], -1).astype(np.float32)


def program(nc, I, out):
    ctx = ExitStack()
    with ctx:
        base = (nc.sbuf_base + 63) // 64 * 64
        limit = nc.sbuf_usable_end

        def at(name, shape, off, dt=F32):
            n = 1
            for s in shape[1:]:
                n *= s
            assert off + 4 * n <= limit, (name, off + 4 * n - limit)
            return nc.alloc_sbuf_tensor_at(name, list(shape), dt, offset=off)

        class Region:

            def __init__(self, start, end=None):
                self.o = start
                self.end = end or limit

            def __call__(self, name, shape, dt=F32):
                n = 1
                for s in shape[1:]:
                    n *= s
                t = at(name, shape, self.o, dt)
                self.o += (4 * n + 31) // 32 * 32
                assert self.o <= self.end, (name, self.o - self.end)
                return t

        fixed = Region(base)
        RAW = [fixed(f"raw{i}", [P, 2048]) for i in range(NRAW)]
        WH = [fixed(f"wh{i}", [P, 1024], F32R) for i in range(NHL)]
        WL = [fixed(f"wl{i}", [P, 1024], F32R) for i in range(NHL)]
        X = fixed("X", [P, 2, D])
        xt0 = fixed.o
        XTH = fixed("XTH", [P, 8, T], F32R)
        XTL = fixed("XTL", [P, 8, T], F32R)
        C = fixed("C", [P, CK])
        CG = fixed("CG", [P, 128 + NV2])
        SM = fixed("SM", [P, 256])
        MODS = fixed("MODS", [P, 72, 2])
        AB = fixed("AB", [P, 40])
        NTMP = 4
        TMP = [fixed(f"TMP{i}", [P, 512]) for i in range(NTMP)]
        GB = fixed("GB", [P, D])
        cT = fixed("cT", [P, 8, 32])
        BA = fixed("BA", [18, 512])
        SG = [fixed(f"SG{i}", [P, 512]) for i in range(2)]
        r0 = fixed.o
        r1 = r0 + 47 * 1024

        f_ = Region(r0, r1)
        HTH = f_("HTH", [P, NF, T], F32R)
        HTL = f_("HTL", [P, NF, T], F32R)
        YF = at("YF", [P, 2, D], r0)
        POS = at("POS", [P, 2, D], xt0)
        a_ = Region(r0, r1)
        qT = a_("qT", [P, 8, T])
        kT = a_("kT", [P, 8, T])
        VA = a_("VA", [P, 2, D])
        OA = a_("OA", [P, 2, D])
        NSA = 8
        SA = [a_(f"SA{i}", [P, 384]) for i in range(NSA)]
        TA = [a_(f"TA{i}", [P, 384]) for i in range(2)]
        LV = at("LV", [P, 256], r0)
        VR = at("VR", [P, 2, P], r0 + 1024)

        c_ = Region(r1)
        XC = c_("XC", [P, 2, D])
        XUH = c_("XUH", [P, 8, T], F32R)
        XUL = c_("XUL", [P, 8, T], F32R)
        r2 = c_.o
        HCH = c_("HCH", [P, 8, T], F32R)
        HCL = c_("HCL", [P, 8, T], F32R)
        YC = at("YC", [P, 2, D], r2)
        GC = c_("GC", [P, D])
        k_ = Region(r2)
        ckv = k_("ckv", [P, 2, D])
        cv = k_("cv", [P, 2, 4, 257])
        BG = k_("BG", [P, 16])
        WG = k_("WG", [P, 8, 16])
        WGH = k_("WGH", [P, 8, 16], F32R)
        WGL = k_("WGL", [P, 8, 16], F32R)
        GT = k_("GT", [P, 2, 16])
        LI = k_("LI", [P, 2, 8])
        LF = k_("LF", [P, 2, 8])
        GS = k_("GS", [P, 12, 16])
        rT = k_("rT", [8, T])
        MST = k_("MST", [P, 24])
        assert k_.o <= c_.o
        CS = at("CS", [P, 2, 8, 257], r1)

        m_ = Region(r0, r1)
        mqT = m_("mqT", [P, 8, T])
        mkT = m_("mkT", [P, 8, T])
        mk = m_("mk", [P, 2, D])
        mv = m_("mv", [P, 2, 4, 257])
        Hm = m_("Hm", [P, 2, D])
        DE = [m_(f"DE{i}", [P, 4, P]) for i in range(2)]
        PPt = [m_(f"PT{i}", [P, P]) for i in range(4)]
        n_ = Region(r1 + 2 * 8 * 257 * 4, r2)
        NUM = [n_(f"NUM{i}", [P, 257]) for i in range(6)]
        bst = n_("bst", [P, 48])
        bag = n_("bag", [P, 16])
        BSR = n_("BSR", [4, P])
        BSC = n_("BSC", [P, 4])
        VV = at("VV", [P, 2, D], r2)
        UU = at("UU", [P, 2, D], r2 + 8192)
        g_ = Region(r0, r0 + 32 * 1024)
        OO = g_("OO", [P, 2, D])
        GAA = g_("GAA", [P, 2, D])
        GBB = g_("GBB", [P, 2, D])
        WST = g_("WST", [P, 4, P])
        WS = g_("WS", [P, 4, P])

        PS = [ctx.enter_context(nc.psum_tensor(f"ps{i}", [P, 512], F32)) for i in range(8)]

        sems = {e: ctx.enter_context(nc.semaphore(f"s_{e}")) for e in ("pe", "act", "dve", "pool")}
        for i in range(NRAW):
            sems[f"raw{i}"] = ctx.enter_context(nc.semaphore(f"s_raw{i}"))
        for n in ("cst", "cst2", "gf", "vec", "x", "ctx", "gb", "lam", "ba", "bg", "wg", "pos", "ws", "bs", "out"):
            sems[n] = ctx.enter_context(nc.semaphore(f"s_{n}"))

        ENG = ("pe", "act", "dve", "pool")
        Q, CNT, SEEN, LAST = {}, {}, {}, {}
        who_emits = ["main"]

        def reset():
            for e in ENG + ("sp",):
                Q[e] = []
                SEEN[e] = {}
            for s in sems:
                CNT[s] = 0
            for st in ("main", "fill"):
                LAST[st] = {}
            who_emits[0] = "main"

        def op(e, f, w=(), inc=1, sem=None):
            for s, v in w:
                if SEEN[e].get(s, 0) < v:
                    SEEN[e][s] = v
                    Q[e].append((None, sems[s], v))
            s = sem or e
            if inc:
                CNT[s] += inc
            Q[e].append((f, sems[s] if inc else None, inc))
            if sem is None:
                LAST[who_emits[0]][e] = (s, CNT[s])
            return (s, CNT[s])

        def fence(*streams):
            return [t for st in (streams or (who_emits[0],)) for t in LAST[st].values()]

        def dma(e, dst, src, sem, w=()):
            return op(e, lambda g: g.dma_start(dst, src), w, 16, sem)

        def mm(o, l, r, start, stop, w=(), inc=0, skip=False):
            return op("pe", lambda g: g.matmul(o, l, r, start=start, stop=stop, skip_group_check=skip), w, inc)

        def tr(o, i, w=(), inc=0):
            n = i.shape[0]
            return op("pe", lambda g: g.transpose(o, i, C[0:n, 0:n]), w, inc)

        def act(o, i, fn, w=(), bias=0.0, scale=1.0, acc=None):
            if acc is None:
                return op("act", lambda g: g.activation(o, i, fn, bias=bias, scale=scale), w)
            return op("act", lambda g: g.activation(o, i, fn, bias=bias, scale=scale, accum_out=acc), w)

        def tt(e, o, a, b, f, w=()):
            return op(e, lambda g: g.tensor_tensor(o, a, b, f), w)

        def ts(e, o, a, s1, s2, f1, f2=None, w=()):
            if f2 is None:
                return op(e, lambda g: g.tensor_scalar(o, a, s1, None, f1), w)
            return op(e, lambda g: g.tensor_scalar(o, a, s1, s2, f1, f2), w)

        def stt(o, a, s, b, f1, f2, w=()):
            return op("dve", lambda g: g.scalar_tensor_tensor(o, a, s, b, f1, f2), w)

        def dot(o, junk, a, b, w=()):
            return op("dve", lambda g: g.tensor_tensor_reduce(junk, a, b, 1.0, 0.0, ALU.mult, ALU.add, o), w)

        def cp(e, o, a, w=()):
            return op(e, lambda g: g.tensor_copy(o, a), w)

        def red(o, a, f, w=(), negate=False):
            if negate:
                return op("dve", lambda g: g.tensor_reduce(o, a, AX, f, negate=True), w)
            return op("dve", lambda g: g.tensor_reduce(o, a, AX, f), w)

        def recip(o, a, w=()):
            return op("dve", lambda g: g.reciprocal(o, a), w)

        def mset(e, o, v, w=()):
            return op(e, lambda g: g.memset(o, v), w)

        def con(name):
            o, w = CC[name]
            return C[:, o:o + w]

        def col(name, k=0):
            o, _ = VEC[name]
            return CG[:, o + k:o + k + 1]

        BANKS = []

        def take():
            return BANKS.pop(0)

        def give(b, t):
            BANKS.append((b, t))

        plan, ST = [], {}
        cutter, deep = ["dve"], [1]

        def stream_reset(known):
            ST.clear()
            ST.update(known=known, got=0, dma=0, split=0, sub=0, raw_free={}, hl_free={}, halves={}, landed={})

        def pump():
            while ST["dma"] < len(ST["known"]) and (ST["dma"] < NRAW or ST["dma"] - NRAW in ST["raw_free"]):
                j = ST["dma"]
                src, nk, nn, split = ST["known"][j]
                s = j % NRAW
                dst = RAW[s][:, 0:nk * nn].rearrange("p (k n) -> p k n", k=nk)
                ST["landed"][j] = dma("sp", dst, src, f"raw{s}", ST["raw_free"].get(j - NRAW, ()))
                ST["dma"] += 1

        def split_chunk(j):
            src, nk, nn, split = ST["known"][j]
            raw = RAW[j % NRAW]
            halves, last = [], None
            n = nk * nn
            cuts = [(0, n // 2), (n // 2, n)] if n > 1024 else [(0, n)]
            for a, b in cuts:
                g = ST["sub"]
                s = g % NHL
                free = ST["hl_free"].get(g - NHL, ())
                h, l = WH[s][:, 0:b - a], WL[s][:, 0:b - a]
                t1 = act(h, raw[:, a:b], ACT.Copy, [ST["landed"][j], *free])
                t2 = tt(cutter[0], l, raw[:, a:b], h.bitcast(F32), ALU.subtract, [t1, ST["landed"][j], *free])
                halves.append((h, l, t1, t2, g))
                ST["sub"] += 1
                last = t2
            ST["halves"][j] = halves
            ST["raw_free"][j] = [last]
            pump()

        def ahead(j):
            k = ST["split"]
            while k < len(ST["known"]) and k <= j:
                if ST["known"][k][3] and k not in ST["halves"]:
                    split_chunk(k)
                k += 1
            while k < len(ST["known"]) and (k in ST["halves"] or not ST["known"][k][3]):
                k += 1
            ST["split"] = k

        def ahead_next(depth=1):
            if ST["known"] is None:
                return
            if sum(j >= ST["got"] for j in ST["halves"]) >= max(depth, deep[0]):
                return
            k = ST["split"]
            while k < len(ST["known"]) and (k in ST["halves"] or not ST["known"][k][3]):
                k += 1
            ST["split"] = k
            g = ST["sub"] + 1 - NHL
            if k < len(ST["known"]) and k not in ST["halves"] and k in ST["landed"] and (g < 0 or g in ST["hl_free"]):
                split_chunk(k)

        def ahead_pool():
            cutter[0] = "pool"
            ahead_next(2)
            cutter[0] = "dve"

        def get(src, nk, nn, split=True):
            j = ST["got"]
            ST["got"] += 1
            if ST["known"] is None:
                plan.append((src, nk, nn, split))
                return None
            assert ST["known"][j][1:] == (nk, nn, split)
            if split:
                ahead(j)
            return j

        def wsrc(wt, k0, nk, n0, nn):
            return wt[k0 * P:(k0 + nk) * P, n0:n0 + nn].rearrange("(k p) n -> p k n", p=P)

        def moving(wt, row0, XH, XL, n0, kts, banks, w, th, nk):
            j = get(wsrc(wt, row0 + kts[0], len(kts), n0, 512), len(kts), 512)
            if j is None:
                return ("pe", 0), ("pe", 0)
            hv = ST["halves"][j]
            per = len(kts) // len(hv)
            toks = [None, None]
            last = kts[-1] == nk - 1
            order = [(i, t) for t in range(2) for i in range(len(hv))]
            for i, t in order if last else sorted(order):
                h, l, t1, t2, g = hv[i]
                hh, ll = h.rearrange("p (k n) -> p k n", k=per), l.rearrange("p (k n) -> p k n", k=per)
                for kk in range(per):
                    k = kts[i * per + kk]
                    a, b = XH[:, k, t * P:t * P + P], XL[:, k, t * P:t * P + P]
                    o = PS[banks[t]][:, :]
                    mm(o, a, hh[:, kk, :], k == 0, False, [t1, *w, *th[k]])
                    mm(o, b, hh[:, kk, :], False, False)
                    toks[t] = mm(o, a, ll[:, kk, :], False, k == nk - 1, [t2], 1 if kk == per - 1 else 0)
                if t == 1:
                    ST["hl_free"][g] = [toks[1]]
            ahead_next()
            return toks

        def stationary(wt, XH, XL, n0, bank, w, th):
            j = get(wsrc(wt, 0, 8, n0, 256), 8, 256)
            if j is None:
                return ("pe", 0)
            hv = ST["halves"][j]
            tok = None
            for f in range(2):
                o = PS[bank][:, f * T:f * T + T]
                for i, (h, l, t1, t2, g) in enumerate(hv):
                    hh, ll = h.rearrange("p (k n) -> p k n", k=4), l.rearrange("p (k n) -> p k n", k=4)
                    for kk in range(4):
                        k = 4 * i + kk
                        a, b = hh[:, kk, f * P:f * P + P], ll[:, kk, f * P:f * P + P]
                        mm(o, a, XH[:, k, :], k == 0, False, [t1, *w, *th[k]])
                        mm(o, a, XL[:, k, :], False, False)
                        tok = mm(o, b, XH[:, k, :], False, k == 7, [t2], 1 if kk == 3 else 0)
                    if f == 1:
                        ST["hl_free"][g] = [tok]
            ahead_next()
            return tok

        def rows_linear(wt, XH, XL, nk, th, done, n_base=0, row0=0, wait=()):
            for n0 in (0, 512):
                (b0, f0), (b1, f1) = take(), take()
                k, tks = 0, None
                while k < nk:
                    m = min(4, nk - k)
                    tks = moving(wt, row0, XH, XL, n_base + n0, list(range(k, k + m)), (b0, b1), [*wait, *f0, *f1],
                                 th, nk)
                    k += m
                    if k < nk:
                        yield 0
                done(0, n0, b0, tks[0])
                done(1, n0, b1, tks[1])
                yield 0

        smc = [0]

        def sm(n):
            if smc[0] + n > 256:
                smc[0] = 0
            a = SM[:, smc[0]:smc[0] + n]
            smc[0] += n
            return a

        tmi = [0]
        TMF = {}

        def tmp():
            assert any(TMF.get(i) != "held" for i in range(NTMP))
            while TMF.get(tmi[0] % NTMP, []) == "held":
                tmi[0] += 1
            i = tmi[0] % NTMP
            tmi[0] += 1
            return i, TMP[i], TMF.get(i, [])

        I32 = mybir.dt.int32

        def rstd(ss, n, count, w):
            v, i, y, a = sm(n), sm(n), sm(n), sm(n)
            tv = ts("dve", v, ss, 1.0 / count, EPS, ALU.mult, ALU.add, w)
            t = op("dve", lambda g: g.tensor_scalar(i.bitcast(I32), v.bitcast(I32), 1, None,
                                                    ALU.logical_shift_right), [tv])
            tv = ts("dve", v, v, -0.5, None, ALU.mult, None, [t])
            t = ts("dve", y.bitcast(I32), i.bitcast(I32), -1.0, 1597463007.0, ALU.mult, ALU.add, [t])
            if n > 2:
                for _ in range(3):
                    t = tt("dve", a, y, y, ALU.mult, [t])
                    t = tt("dve", a, a, v, ALU.mult, [t, tv])
                    t = stt(y, a, 1.5, y, ALU.add, ALU.mult, [t])
                return y, t
            tc = [[t, tv]] * n
            for _ in range(3):
                tc = [[stt(a[:, c:c + 1], y[:, c:c + 1], v[:, c:c + 1], y[:, c:c + 1], ALU.mult, ALU.mult, tc[c])]
                      for c in range(n)]
                tc = [[stt(y[:, c:c + 1], a[:, c:c + 1], 1.5, y[:, c:c + 1], ALU.add, ALU.mult, tc[c])]
                      for c in range(n)]
            return y, tc[-1][0]

        def to_halves(src, H, L, scale, shift, w, wfree, blocks=range(0, 8, 2)):
            th = {}
            for k in blocks:
                b, f = take()
                for kk in range(2):
                    for t in range(2):
                        tk = tr(PS[b][:, kk * T + t * P:kk * T + t * P + P], src(t, k + kk), [*w, *f],
                                1 if kk == 1 and t == 1 else 0)
                i, tm, fr = tmp()
                for kk in range(2):
                    t1 = act(tm[:, kk * T:kk * T + T], PS[b][:, kk * T:kk * T + T], ACT.Identity, [tk, *fr, *w],
                             bias=shift(k + kk), scale=scale(k + kk))
                give(b, [t1])
                tv = tm[:, :].rearrange("p (k t) -> p k t", k=2)
                h, l = H[:, k:k + 2, :], L[:, k:k + 2, :]
                t2 = cp("dve", h, tv, [t1, *wfree])
                t3 = tt("pool" if k % 4 == 2 else "dve", l, tv, h.bitcast(F32), ALU.subtract, [t1, t2, *wfree])
                TMF[i] = [t2, t3]
                th[k] = th[k + 1] = [t2, t3]
            return th

        def normed(x, w, Y, wy, eng="act"):
            ss = sm(2)
            t1 = dot(ss[:, 0:1], Y[:, 0, :], x[:, 0, :], x[:, 0, :], [*w, *wy])
            if eng == "dve":
                t2 = dot(ss[:, 1:2], Y[:, 1, :], x[:, 1, :], x[:, 1, :], [*w, *wy])
            else:
                t2 = act(Y[:, 1, :], x[:, 1, :], ACT.Square, [*w, *wy], acc=ss[:, 1:2])
            r, t = rstd(ss, 2, D, [t1, t2])
            ta = ts("dve", Y[:, 0, :], x[:, 0, :], r[:, 0:1], None, ALU.mult, None, [t])
            tb = act(Y[:, 1, :], x[:, 1, :], ACT.Copy, [t], scale=r[:, 1:2])
            return [ta, tb]

        def load_gb(v, w):
            return dma("pool", GB[:, :], v.partition_broadcast(P), "gb", w)

        def keep_sums(held, ss):
            def d_(tile, n0, bank, tok):
                i_, tm, fr = tmp()
                c = tile + n0 // 256
                t1 = act(tm[:, :], PS[bank][:, :], ACT.Square, [tok, *fr], acc=ss[:, c:c + 1])
                TMF[i_] = [t1]
                held.append((tile, n0, bank, tok, t1))
            return d_

        def post_add(held, ss, gtok, x, wx):
            s2 = sm(2)
            t = tt("dve", s2, ss[:, 0:2], ss[:, 2:4], ALU.add, [h[4] for h in held])
            ahead_pool()
            r, t = rstd(s2, 2, D, [t])
            res = []
            for tile, n0, bank, tok, t1 in sorted(held, key=lambda h: (-h[0], h[1])):
                i_, tm, fr = tmp()
                ta = stt(tm[:, :], PS[bank][:, :], r[:, tile:tile + 1], GB[:, n0:n0 + 512], ALU.mult, ALU.mult,
                         [t, tok, gtok, *fr])
                give(bank, [ta])
                xs = x[:, tile, n0:n0 + 512]
                tb = tt("dve", xs, xs, tm[:, :], ALU.add, [ta, *wx])
                TMF[i_] = [tb]
                res.append(tb)
            return res

        SGF = {}
        sgi = [0]

        def silu_tile():
            while SGF.get(sgi[0] % 2) == "held":
                assert SGF.get((sgi[0] + 1) % 2) != "held"
                sgi[0] += 1
            i = sgi[0] % 2
            sgi[0] += 1
            free, SGF[i] = SGF.get(i, []), "held"
            return i, free

        def hidden(w_in, XH, XL, th, H, L, pairs, h0, wreg, hs):
            for c in pairs:
                bg, fg = take()
                tg = stationary(w_in, XH, XL, 256 * c, bg, fg, th)
                i, sgf = silu_tile()
                sg = SG[i][:, :]
                ta = act(sg, PS[bg][:, :], ACT.Silu, [tg, *sgf, *wreg])
                give(bg, [ta])
                yield 0
                bu, fu = take()
                tu = stationary(w_in, XH, XL, DFF + 256 * c, bu, fu, th)
                i_, tm, fr = tmp()
                t2 = tt("dve", tm[:, :], PS[bu][:, :], sg, ALU.mult, [ta, tu, *fr])
                give(bu, [t2])
                SGF[i] = [t2]
                tv = tm[:, :].rearrange("p (k t) -> p k t", k=2)
                k = 2 * c - h0
                h, l = H[:, k:k + 2, :], L[:, k:k + 2, :]
                t3 = act(h, tv, ACT.Copy, [t2, *wreg])
                t4 = tt("pool", l, tv, h.bitcast(F32), ALU.subtract, [t3, *wreg])
                TMF[i_] = [t3, t4]
                hs[k] = hs[k + 1] = [t3, t4]
                yield 0

        def ffn(w_in, w_down, th, wreg, done, between=None):
            hs = {}
            yield from hidden(w_in, XTH, XTL, th, HTH, HTL, range(11), 0, wreg, hs)
            if between is not None:
                between()
            yield from rows_linear(w_down, HTH, HTL, NF, hs, done)

        def skew(units, depth):
            live, todo = [], list(units)
            while live or todo:
                if todo and len(live) < depth:
                    live.append(todo.pop(0))
                for g in list(live):
                    if next(g, "end") == "end":
                        live.remove(g)
                yield "tick"

        def pairs(units):
            def pair(a, b):
                for part in a:
                    next(b)
                    if part != "part":
                        yield 0
                next(b, 0)
            return [pair(units[i], units[i + 1]) for i in range(0, len(units), 2)]

        def gain(name, off=0):
            return lambda k: col(name, off + k)

        def zero(k):
            return 0.0

        def one(k):
            return 1.0

        SHARED = {}

        def ada_steps():
            wa = I["w_ada_2"][0]
            pend = None

            def columns(n, i_, tm, t1):
                b, f = take()
                for z in range(4):
                    tk = mm(PS[b][:, 2 * z:2 * z + 2], tm[:, z * P:z * P + P], con("sel"), True, True, [t1, SHARED["cst"], *f],
                            1 if z == 3 else 0)
                TMF[i_] = [tk]
                t2 = cp("dve", MODS[:, 4 * n:4 * n + 4, :].rearrange("p a b -> p (a b)"), PS[b][:, 0:8], [tk])
                give(b, [t2])
                SHARED["mods"].append(t2)

            for n in range(18):
                b, f = take()
                mm(PS[b][0:32, :], C[0:18, n:n + 1].to_broadcast([18, 32]), BA[:, :], True, False,
                   [SHARED["ba"], *f], 0, True)
                tk = ("pe", 0)
                for half in range(2):
                    j = get(wsrc(wa, 4 * half, 4, 512 * n, 512), 4, 512, False)
                    if j is None:
                        continue
                    raw = RAW[j % NRAW][:, :].rearrange("p (k n) -> p k n", k=4)
                    for kk in range(4):
                        tk = mm(PS[b][32 * kk:32 * kk + 32, :], cT[:, 4 * half + kk, :], raw[:, kk, :],
                                half == 0 and kk > 0, half == 1, [ST["landed"][j], SHARED["ct"]],
                                1 if kk == 3 else 0, True)
                    ST["raw_free"][j] = [tk]
                    pump()
                    ahead_next()
                if pend is not None:
                    columns(*pend)
                i_, tm, fr = tmp()
                t1 = act(tm[:, :], PS[b][:, :], ACT.Copy, [tk, *fr])
                give(b, [t1])
                TMF[i_] = "held"
                pend = (n, i_, tm, t1)
                yield 0
            columns(*pend)
            yield 0

        def need_mods(v):
            while len(SHARED["mods"]) < 2 * v + 2:
                next(SHARED["ada"])
            return SHARED["mods"][2 * v:2 * v + 2]

        def modcols(name, v, who, w):
            m = need_mods(v) + need_mods(v + 1)
            t = stt(AB[:, 8 * who:8 * who + 8], MODS[:, 8 * (v + 1):8 * (v + 1) + 8, who], 1.0,
                    CG[:, VEC[name][0]:VEC[name][0] + 8], ALU.add, ALU.mult, [*m, *w, SHARED["cg"]])
            return (lambda k: AB[:, 8 * who + k:8 * who + k + 1], lambda k: MODS[:, 8 * v + k, who:who + 1], t)

        def gate_rows(v, who, fac, G, w):
            m = need_mods(v)
            res = []
            for half in range(2):
                i_, tm, fr = tmp()
                b, f = take()
                for z in range(4):
                    k = 4 * half + z
                    t1 = ts("dve", tm[:, z * P:z * P + P], con("id"), MODS[:, 8 * v + k, who:who + 1], fac, ALU.mult,
                            ALU.mult, [*m, *fr])
                tk = mm(PS[b][:, :], con("one"), tm[:, :], True, True, [t1, *f], 1)
                TMF[i_] = [tk]
                t2 = act(G[:, 512 * half:512 * half + 512], PS[b][:, :], ACT.Copy, [tk, *w])
                give(b, [t2])
                res.append(t2)
            return res

        def gated(G, gtok, x, xw, res):
            def d_(tile, n0, bank, tok):
                i_, tm, fr = tmp()
                t1 = tt("dve", tm[:, :], PS[bank][:, :], G[:, n0:n0 + 512], ALU.mult, [tok, *fr, *gtok])
                give(bank, [t1])
                xs = x[:, tile, n0:n0 + 512]
                t2 = tt("dve" if n0 else "pool", xs, xs, tm[:, :], ALU.add, [t1, *xw])
                TMF[i_] = [t2]
                res[(tile, n0)] = t2
            return d_

        def conv_feats(win, n0, base_ft, XH, XL, dstT, scale, th, wdst, kc, res, late=None):
            def to_rows(i, rows, t3, i_):
                b, f = take()
                for f2 in range(2):
                    for t_ in range(2):
                        tk = tr(PS[b][:, t_ * 256 + f2 * P:t_ * 256 + f2 * P + P],
                                rows[:, f2 * T + t_ * P:f2 * T + t_ * P + P], [t3, *f],
                                1 if f2 == 1 and t_ == 1 else 0)
                if i_ is not None:
                    TMF[i_] = [tk]
                t4 = act(kc[:, :, 256 * i:256 * i + 256], PS[b][:, :].rearrange("p (t d) -> p t d", t=2),
                         ACT.Copy, [tk, *wdst])
                give(b, [t4])
                res.append(t4)

            pend = None
            for i in range(4):
                b, f = take()
                tk = stationary(win, XH, XL, n0 + 256 * i, b, f, th)
                i_, tm, fr = tmp()
                for f2 in range(2):
                    ft = base_ft + 2 * i + f2
                    o, z = tm[:, f2 * T:f2 * T + T], f2 * T
                    ta = ts("dve", o, PS[b][:, z:z + 256], col("conv_qk_w_2", 16 + ft), col("conv_qk_b_2", ft),
                            ALU.mult, ALU.add, [tk, *fr])
                    ta = stt(o[:, 1:256], PS[b][:, z:z + 255], col("conv_qk_w_2", ft), o[:, 1:256], ALU.mult,
                             ALU.add, [ta])
                    ta = stt(o[:, 0:255], PS[b][:, z + 1:z + 256], col("conv_qk_w_2", 32 + ft), o[:, 0:255],
                             ALU.mult, ALU.add, [ta])
                give(b, [ta])
                if dstT is not None:
                    dst = dstT[:, 2 * i:2 * i + 2, :].rearrange("p k t -> p (k t)")
                    t3 = act(dst, tm[:, :], ACT.Silu, [ta, *wdst])
                    TMF[i_] = [t3]
                    if scale != 1.0:
                        t3 = ts("pool", dst, dst, scale, None, ALU.mult, None, [t3])
                    rows = dst
                else:
                    t3 = act(tm[:, :], tm[:, :], ACT.Silu, [ta])
                    rows = tm[:, :]
                res.append(t3)
                if kc is not None:
                    if pend is not None:
                        to_rows(*pend)
                    pend = (i, rows, t3, i_ if dstT is None else None)
                    if dstT is None:
                        TMF[i_] = "held"
                yield 0
            if pend is not None:
                late.append(lambda: to_rows(*pend))

        def values(win, XH, XL, th, V, wdst, res):
            def d_(tile, n0, bank, tok):
                t1 = act(V[:, tile, n0 // 256:n0 // 256 + 2, 0:256],
                         PS[bank][:, :].rearrange("p (h d) -> p h d", h=2), ACT.Copy, [tok, *wdst])
                give(bank, [t1])
                res.append(t1)
            yield from rows_linear(win, XH, XL, 8, th, d_, n_base=2048)

        def gates(XH, XL, th, w):
            b, f = take()
            tw1, tw2 = SHARED["wg"]
            o = PS[b][0:16, 0:256]
            for k in range(8):
                mm(o, WGH[:, k, :], XH[:, k, :], k == 0, False, [*th[k], tw1, tw2, *f])
                mm(o, WGL[:, k, :], XH[:, k, :], False, False)
                tk = mm(o, WGH[:, k, :], XL[:, k, :], False, k == 7, (), 1 if k == 7 else 0)
            i_, tm, fr = tmp()
            t0 = cp("dve", tm[0:16, 0:256], o, [tk, *fr])
            give(b, [t0])
            TMF[i_] = "held"
            yield 0
            b, f = take()
            for t_ in range(2):
                tk = tr(PS[b][:, 16 * t_:16 * t_ + 16], tm[0:16, t_ * P:t_ * P + P], [t0, *f], t_)
            TMF[i_] = [tk]
            t1 = tt("dve", GT[:, :, :], PS[b][:, 0:32].rearrange("p (t c) -> p t c", t=2),
                    BG[:, :].unsqueeze(1).to_broadcast([P, 2, 16]), ALU.add, [tk, SHARED["bg"], *w])
            give(b, [t1])
            yield 0
            g4 = GT[:, :, :].rearrange("p t (d z h) -> p t d z h", d=2, z=2)
            li = LI[:, :, :].rearrange("p t (d h) -> p t d h", d=2)
            lf = LF[:, :, :].rearrange("p t (d h) -> p t d h", d=2)
            t2 = cp("dve", li, g4[:, :, :, 0, :], [t1])
            t3 = cp("dve", lf, g4[:, :, :, 1, :], [t1])
            f16 = LF[:, :, :].rearrange("p t c -> p (t c)")
            t4 = act(GS[:, 0, :], f16, ACT.Abs, [t3])
            t4 = act(GS[:, 0, :], GS[:, 0, :], ACT.Exp, [t4], scale=-1.0)
            t4 = act(GS[:, 0, :], GS[:, 0, :], ACT.Ln, [t4], bias=1.0)
            t5 = stt(f16, f16, 0.0, GS[:, 0, :], ALU.min, ALU.subtract, [t4])
            yield 0
            b, f = take()
            z = PS[b]
            for t_ in range(2):
                mm(z[:, 8 * t_:8 * t_ + 4], con("tle"), LF[:, t_, 0:4], True, True, [t5, *f])
                mm(z[:, 8 * t_ + 4:8 * t_ + 8], con("tge"), LF[:, t_, 4:8], True, True)
                tk = mm(z[:, 16 + 8 * t_:24 + 8 * t_], con("one"), LF[:, t_, :], True, True, (), 1)
            t6 = cp("dve", GS[:, 1:3, :].rearrange("p a b -> p (a b)"), z[:, 0:32], [tk])
            give(b, [t6])
            t7 = tt("dve", GS[:, 3, :], LI[:, :, :].rearrange("p t c -> p (t c)"), GS[:, 1, :], ALU.subtract,
                    [t6, t2])
            yield 0
            b, f = take()
            for t_ in range(2):
                tk = tr(PS[b][0:8, t_ * P:t_ * P + P], GS[:, 3, 8 * t_:8 * t_ + 8], [t7, *f], 1)
            t8 = cp("dve", rT[:, :], PS[b][0:8, 0:256], [tk])
            give(b, [t8])
            t9 = red(GS[0:8, 4, 0:2], rT[:, :].rearrange("p (t s) -> p t s", t=2), ALU.max, [t8])
            for t_ in range(2):
                t9 = ts("dve", GS[0:8, 5, 8 * t_:8 * t_ + 8], C[0:8, 0:8], GS[0:8, 4, t_:t_ + 1], None,
                        ALU.mult, None, [t9])
            yield 0
            b, f = take()
            o1 = CC["one"][0]
            tk = mm(PS[b][:, 0:16], C[0:8, o1:o1 + P], GS[0:8, 5, :], True, True, [t9, *f], 1)
            t10 = cp("dve", GS[:, 6, :], PS[b][:, 0:16], [tk])
            give(b, [t10])
            SHARED["gates"] = [t7, t8, t10, t6]
            yield 0

        def mx_step(d, t_, w):
            s = slice(8 * t_ + 4 * d, 8 * t_ + 4 * d + 4)
            m, mxx = MST[:, 4 * d:4 * d + 4], MST[:, 8 + 4 * d:12 + 4 * d]
            t = tt("dve", mxx, m, GS[:, 6, s], ALU.max, w)
            ta = tt("dve", GS[:, 7, s], m, mxx, ALU.subtract, [t])
            tb = tt("dve", GS[:, 8, s], GS[:, 3, s], mxx, ALU.subtract, [t])
            tn_ = tt("dve", m, GS[:, 2, s], mxx, ALU.add, [t, ta])
            ta = act(GS[:, 7, s], GS[:, 7, s], ACT.Exp, [ta])
            tb = act(GS[:, 8, s], GS[:, 8, s], ACT.Exp, [tb])
            return [ta, tb, tn_]

        def update(d, t_, h, K, V, w, first, cs):
            c = 8 * t_ + 4 * d + h
            i, fr = silu_tile()
            tm = SG[i]
            t1 = act(tm[:, 0:257], V[:, t_, h, :], ACT.Copy, [*w, *fr], scale=GS[:, 8, c:c + 1])
            yield 0
            for z in range(2):
                b, f = take()
                tk = mm(PS[b][:, 0:257], K[:, t_, h * 256 + z * P:h * 256 + z * P + P], tm[:, 0:257], True, True,
                        [t1, *w, *f], 1)
                dst = CS[:, z, 4 * d + h, :]
                if first:
                    t2 = cp("dve", dst, PS[b][:, 0:257], [tk, *w])
                else:
                    t2 = stt(dst, dst, GS[:, 7, c:c + 1], PS[b][:, 0:257], ALU.mult, ALU.add,
                             [tk, *w, *cs.get((d, h), [])])
                give(b, [t2])
                cs[(d, h)] = [t2]
            SGF[i] = [tk]

        def context_stream():
            tctx = dma("pool", XC[:, :, :], I["ctx_2"][0].rearrange("(t p) d -> p t d", p=P), "ctx")
            while len(SHARED["mods"]) < 6:
                next(SHARED["ada"])
                yield 1
            sc, sh, t = modcols("g_ffn1_2", 0, 1, [])
            tn = normed(XC, [tctx], YC, [])
            yield 0
            th = to_halves(lambda t_, k: YC[:, t_, k * P:k * P + P], XUH, XUL, sc, sh, [*tn, t], [])
            yield 0
            gt = gate_rows(2, 1, 0.5, GC, fence())
            yield 0
            res = {}
            for h0, h1 in ((0, 8), (8, 16), (16, 22)):
                hs = {}
                wreg = fence()
                yield from hidden(I["w_ffn1_in_2"][0], XUH, XUL, th, HCH, HCL, range(h0 // 2, h1 // 2), h0, wreg, hs)
                yield from rows_linear(I["w_ffn1_out_2"][0], HCH, HCL, h1 - h0, hs,
                                       gated(GC, gt, XC, [tctx, *tn, *res.values()], res), row0=h0)
            while len(SHARED["mods"]) < 10:
                next(SHARED["ada"])
                yield 1
            win = I["w_in_2"][0]
            SHARED["bg"] = dma("pool", BG[:, :], I["b_gates_2"][0].partition_broadcast(P), "bg", fence())
            twg = dma("pool", WG[:, :, :], win[:, 3072:3088].rearrange("(k p) n -> p k n", p=P), "wg", fence())
            sc, sh, t = modcols("g_mix_2", 3, 1, fence())
            tn = normed(XC, list(res.values()), YC, fence())
            yield 0
            yield 0
            th = to_halves(lambda t_, k: YC[:, t_, k * P:k * P + P], XUH, XUL, sc, sh, [*tn, t], fence())
            w1 = fence()
            yield 0
            t1 = mset("pool", cv[:, :, :, 256:257], 1.0, w1)
            t2 = mset("pool", MST[:, :], 0.0, w1)
            tw1 = cp("dve", WGH[:, :, :], WG[:, :, :], [twg, *w1])
            tw2 = tt("dve", WGL[:, :, :], WG[:, :, :], WGH[:, :, :].bitcast(F32), ALU.subtract, [tw1])
            SHARED["wg"] = (tw1, tw2)
            res = [t1, t2]
            yield from gates(XUH, XUL, th, w1)
            late = []
            yield from conv_feats(win, 1024, 8, XUH, XUL, None, 1.0, th, w1, ckv, res, late)
            for _ in values(win, XUH, XUL, th, cv, w1, res):
                while late:
                    late.pop()()
                yield 0
            su, cs = [*res, *SHARED["gates"], *fence()], {}
            for s_ in range(2):
                a = [(d, s_ if d == 0 else 1 - s_) for d in range(2)]
                w = [mx_step(d, t_, [*su, *SHARED.get("mxw", [])]) for d, t_ in a]
                un = [update(d, t_, h, ckv, cv, [*su, *w[d]], s_ == 0, cs) for d, t_ in a for h in range(4)]
                for _ in skew(pairs(un), 2):
                    yield 1
                su = su + [t for v in w for t in v]
            SHARED["states"] = su + [t for v in cs.values() for t in v]
            while True:
                if next(SHARED["ada"], "end") == "end":
                    break
                yield 1

        def gap(n, last=False):
            cutter[0] = "pool"
            for i in range(n):
                deep[0] = 1 if last and i == n - 1 else 2
                yield 1
            cutter[0] = "dve"
            deep[0] = 1

        def attention_a_head(h, st):
            lam, tlam, w_qkv = st["lam"], st["tlam"], st["w"]
            sc = []
            for a in range(2):
                b, f = take()
                q_, k_ = qT[64 * a:64 * a + 64, h, :], kT[64 * a:64 * a + 64, h, :]
                mm(PS[b][:, 0:256], q_[:, 128:256], k_, True, True, [*w_qkv, *f])
                tk = mm(PS[b][:, 256:384], q_[:, 0:128], k_[:, 0:128], True, True, (), 1)
                sc.append((b, tk))
            rs = []
            for a in range(2):
                b, tk = sc[a]
                i = (2 * h + a) % NSA
                S_ = SA[i]
                t1 = stt(S_[:, :], PS[b][:, 0:384], 0.125, con("mka"), ALU.mult, ALU.add, [tk, *st["sf"].get(i, [])])
                give(b, [t1])
                nm, ls, rl = sm(2), sm(2), sm(2)
                t2 = red(nm[:, 0:1], S_[:, 0:256], ALU.max, [t1], negate=True)
                t3 = red(nm[:, 1:2], S_[:, 256:384], ALU.max, [t1], negate=True)
                t4 = act(S_[:, 0:256], S_[:, 0:256], ACT.Exp, [t2, t1], bias=nm[:, 0:1], acc=ls[:, 0:1])
                t5 = act(S_[:, 256:384], S_[:, 256:384], ACT.Exp, [t3, t1], bias=nm[:, 1:2], acc=ls[:, 1:2])
                rs.append((i, rl, ls, [t4, t5]))
            yield "part"
            for a in range(2):
                i, rl, ls, w = rs[a]
                t6 = recip(rl, ls, w)
                if a == 1:
                    t6 = ts("dve", rl, rl, lam, None, ALU.mult, None, [t6, tlam])
                w.append(t6)
            i0, r0_, _, w0 = rs[0]
            i1, r1_, _, w1 = rs[1]
            tks = []
            for c, (lo, hi) in enumerate([(0, 256), (256, 384)]):
                t7 = ts("dve", SA[i1][:, lo:hi], SA[i1][:, lo:hi], r1_[:, c:c + 1], None, ALU.mult,
                        None, w1)
                t8 = stt(SA[i0][:, lo:hi], SA[i0][:, lo:hi], r0_[:, c:c + 1], SA[i1][:, lo:hi], ALU.mult,
                         ALU.subtract, [*w0, t7])
                tks.append(t8)
            st["sf"][i1] = tks
            yield 0
            b, f = take()
            tr(PS[b][:, 0:128], SA[i0][:, 256:384], [*tks, *f])
            tr(PS[b][:, 128:256], SA[i0][:, 0:128])
            tk = tr(PS[b][:, 256:384], SA[i0][:, 128:256], (), 1)
            st["sf"][i0] = [tk]
            t9 = act(TA[h % 2][:, :], PS[b][:, 0:384], ACT.Copy, [tk, *st["tf"].get(h % 2, [])])
            give(b, [t9])
            yield 0
            b, f = take()
            v0, v1 = VA[:, 0, h * P:h * P + P], VA[:, 1, h * P:h * P + P]
            mm(PS[b][:, 0:128], TA[h % 2][:, 0:128], v0, True, True, [t9, *st["v"], *f])
            mm(PS[b][:, 128:256], TA[h % 2][:, 128:256], v0, True, False)
            tk = mm(PS[b][:, 128:256], TA[h % 2][:, 256:384], v1, False, True, (), 1)
            st["tf"][h % 2] = [tk]
            t1 = act(OA[:, :, h * P:h * P + P], PS[b][:, 0:256].rearrange("p (t d) -> p t d", t=2), ACT.Copy,
                     [tk, *st["ow"]])
            give(b, [t1])
            i_, tm, fr = tmp()
            tt_ = []
            for t in range(2):
                tt_.append(dot(st["oss"][:, 2 * h + t:2 * h + t + 1], tm[:, t * P:t * P + P],
                               OA[:, t, h * P:h * P + P], OA[:, t, h * P:h * P + P], [t1, *fr]))
            TMF[i_] = tt_
            st["o"] += [t1, *tt_]

        def attention_b_head(hd, st):
            h, a = hd // 2, hd % 2
            mlt = con("mlt")
            q_, k_ = qT[64 * a:64 * a + 64, h, :], kT[64 * a:64 * a + 64, h, :]
            b, f = take()
            o = PS[b]
            mm(o[:, 0:256], k_[:, 0:128], q_, True, False, [*st["w"], *f], 0, True)
            tk = mm(o[:, 256:384], k_[:, 128:256], q_[:, 128:256], False, True, (), 1, True)
            i = (2 * hd) % NSA
            S_, P_ = SA[i], SA[i + 1]
            t1 = act(S_[:, :], o[:, 0:384], ACT.Abs, [tk, *st["sf"].get(i, [])])
            t2 = act(S_[:, :], S_[:, :], ACT.Exp, [t1], scale=-1.0)
            yield "part"
            t3 = act(S_[:, :], S_[:, :], ACT.Ln, [t2], bias=1.0)
            t4 = stt(P_[:, :], o[:, 0:384], 0.0, S_[:, :], ALU.max, ALU.add, [t3, *st["sf"].get(i + 1, [])])
            t5 = tt("dve", P_[:, 0:128], P_[:, 0:128], mlt, ALU.mult, [t4])
            t6 = tt("pool", P_[:, 256:384], P_[:, 256:384], mlt, ALU.mult, [t4])
            yield 0
            mm(o[:, 0:256], con("ngt"), P_[:, 0:256], False, False, [t4, t5, t6], 0, True)
            mm(o[:, 128:256], con("neg"), P_[:, 256:384], False, True, (), 0, True)
            tk = mm(o[:, 256:384], con("ngt"), P_[:, 256:384], False, True, (), 1, True)
            st["sf"][i + 1] = [tk]
            t7 = act(S_[:, :], o[:, 0:384], ACT.Exp, [tk, t4])
            give(b, [t7])
            t8 = tt("dve", S_[:, 0:128], S_[:, 0:128], mlt, ALU.mult, [t7])
            t9 = tt("pool", S_[:, 256:384], S_[:, 256:384], mlt, ALU.mult, [t7])
            yield 0
            if hd % 4 == 0:
                st["ob"] = take()
            ob, of = st["ob"]
            v0, v1 = VA[:, 0, hd * 64:hd * 64 + 64], VA[:, 1, hd * 64:hd * 64 + 64]
            c0 = (hd % 4) * 64
            mm(PS[ob][:, c0:c0 + 64], S_[:, 0:128], v0, True, True, [t8, t9, *st["v"], *of])
            mm(PS[ob][:, 256 + c0:256 + c0 + 64], S_[:, 128:256], v0, True, False)
            tk = mm(PS[ob][:, 256 + c0:256 + c0 + 64], S_[:, 256:384], v1, False, True, (), 1)
            st["sf"][i] = [tk]
            if hd % 4 == 3:
                g4 = hd // 4
                t1 = act(OA[:, :, g4 * 256:g4 * 256 + 256], PS[ob][:, :].rearrange("p (t d) -> p t d", t=2),
                         ACT.Copy, [tk])
                give(ob, [t1])
                st["o"].append(t1)

        def scan_start(s_, d, st):
            t_ = s_ if d == 0 else 1 - s_
            sl_ = slice(8 * t_ + 4 * d, 8 * t_ + 4 * d + 4)
            m, M = MST[:, 4 * d:4 * d + 4], MST[:, 16 + 4 * d:20 + 4 * d]
            E, ga, gb = DE[d], GS[:, 11 if d else 9, :], GS[:, 5 if d else 10, :]
            b, f = take()
            for h in range(4):
                j = 4 * d + h
                tk = mm(PS[b][:, h * P:h * P + P], C[0:8, j:j + 1].to_broadcast([8, P]),
                        rT[:, t_ * P:t_ * P + P], True, True, [*st["w"], *f], 1 if h == 3 else 0)
            o3 = CC["mka"][0]
            msk = (con("mb") if d else C[:, o3 + P:o3 + 2 * P]).unsqueeze(1).to_broadcast([P, 4, P])
            t1 = tt("dve", E[:, :, :], PS[b][:, :].rearrange("p (h s) -> p h s", h=4), msk, ALU.add,
                    [tk, *st["h"][d]])
            give(b, [t1])
            t2 = red(M, E[:, :, :], ALU.max, [t1])
            t3 = tt("dve", M, M, m, ALU.max, [t2, *st["su"]])
            t4 = tt("dve", ga[:, 0:4], m, M, ALU.subtract, [t3])
            t5 = stt(ga[:, 4:8], GS[:, 1, sl_], -1.0, M, ALU.mult, ALU.subtract, [t3])
            t6 = ts("dve", ga[:, 8:12], M, -1.0, None, ALU.mult, None, [t3])
            t7 = act(gb[:, 0:8], ga[:, 0:8], ACT.Exp, [t4, t5, *st["h"][d]])
            tD = [act(E[:, h, :], E[:, h, :], ACT.Exp, [t6, t2], bias=ga[:, 8 + h:9 + h]) for h in range(4)]
            st["m"][d] = [t3, t4, t5]
            return tD, t7, gb

        def scan_head(s_, d, h, tD, t7, gb, wu, new, st):
            t_ = s_ if d == 0 else 1 - s_
            i, n4 = 2 * (h % 2) + d, 2 * (h % 3) + d
            b, f = take()
            for z in range(2):
                tk = mm(PS[b][:, 0:P], mqT[:, 2 * h + z, t_ * P:t_ * P + P],
                        mkT[:, 2 * h + z, t_ * P:t_ * P + P], z == 0, z == 1, [*st["w"], *f], 1 if z else 0)
            E = DE[d][:, h, :]
            t8 = tt("dve", E, PS[b][:, 0:P], E, ALU.mult, [tk, tD])
            give(b, [t8])
            b2, f2 = take()
            for z in range(2):
                tn2 = mm(PS[b2][:, 0:257], mqT[:, 2 * h + z, t_ * P:t_ * P + P], CS[:, z, 4 * d + h, :], z == 0,
                         z == 1, [*st["su"], *st["cs"].get((d, h), []), *f2], 1 if z else 0)
            N_ = NUM[n4]
            ta = act(N_[:, :], PS[b2][:, 0:257], ACT.Copy, [tn2, t7, *st["pf"].get(("n", n4), [])],
                     scale=gb[:, h:h + 1])
            give(b2, [ta])
            up = None
            if s_ == 0:
                up = update(d, t_, h, mk, mv, [*wu, *st["w"], tn2], False, st["cs"])
                next(up)
            yield 0
            b, f = take()
            tk = tr(PS[b][:, 0:P], E, [t8, *f], 1)
            t9 = act(PPt[i][:, :], PS[b][:, 0:P], ACT.Copy, [tk, *st["pf"].get(i, [])])
            give(b, [t9])
            if up is not None:
                next(up, 0)
            yield 0
            b, f = take()
            tn1 = mm(PS[b][:, 0:257], PPt[i][:, :], mv[:, t_, h, :], True, True, [t9, *f], 1)
            tb = tt("dve", N_[:, :], PS[b][:, 0:257], N_[:, :], ALU.add, [tn1, ta])
            give(b, [tb])
            st["pf"][i] = [tn1]
            dn, rc = sm(1), sm(1)
            tb = stt(dn, N_[:, 256:257], -1.0, N_[:, 256:257], ALU.mult, ALU.max, [tb])
            tb = tt("dve", dn, dn, gb[:, 4 + h:5 + h], ALU.max, [tb])
            tb = recip(rc, dn, [tb])
            ho = Hm[:, t_, 256 * h:256 * h + 256]
            if s_ == 0:
                tc2 = ts("dve", ho, N_[:, 0:256], rc, None, ALU.mult, None, [tb, *st["w"]])
            else:
                tc2 = stt(ho, N_[:, 0:256], rc, ho, ALU.mult, ALU.add, [tb])
            st["pf"][("n", n4)] = [tc2]
            new += [tc2, tk]

        def main_stream():
            tx = SHARED["x"]
            wq = I["a_w_qkv"][0]
            tc, tcg = SHARED["cst"], SHARED["cg"]
            tn = SHARED["tn"]
            th = to_halves(lambda t, k: OA[:, t, k * P:k * P + P], XTH, XTL, gain("mix_pre_g"), zero, [*tn, tcg], [])
            qk_done, v_done = [], []
            v2 = lambda a: a.rearrange("p (k t) -> p k t", k=2)
            cosb = GB[:, 0:T].unsqueeze(1).to_broadcast([P, 2, T])
            sinb = GB[:, T:2 * T].unsqueeze(1).to_broadcast([P, 2, T])
            lam = AB[:, 32:33]

            def rotate(dst, t1):
                b, f = take()
                t2 = mm(PS[b][:, :], con("rot"), dst, True, True, [t1, tc, *f], 1)
                i_, tm, fr = tmp()
                t3 = tt("dve", v2(tm[:, :]), v2(PS[b][:, :]), sinb, ALU.mult, [t2, SHARED["rot"], *fr])
                give(b, [t3])
                t4 = tt("pool", v2(dst), v2(dst), cosb, ALU.mult, [t2, t1, SHARED["rot"]])
                t5 = tt("pool", dst, dst, tm[:, :], ALU.add, [t3, t4])
                TMF[i_] = [t5]
                qk_done.append(t5)

            pend = None
            for i in range(8):
                b, f = take()
                tk = stationary(wq, XTH, XTL, 256 * i, b, f, th)
                if i == 0:
                    SHARED["small"]()
                    wlv = SHARED["lvdone"]
                if pend is not None:
                    rotate(*pend)
                dst = (qT if i < 4 else kT)[:, 2 * (i % 4):2 * (i % 4) + 2, :].rearrange("p k t -> p (k t)")
                t1 = act(dst, PS[b][:, :], ACT.Copy, [tk, *wlv])
                give(b, [t1])
                pend = (dst, t1)
                yield FQ[i]

            def dv(tile, n0, bank, tok):
                t1 = act(VA[:, tile, n0:n0 + 512], PS[bank][:, :], ACT.Copy, [tok, *SHARED.get("vw", [])])
                give(bank, [t1])
                v_done.append(t1)

            g = rows_linear(wq, XTH, XTL, 8, th, dv, n_base=2048)
            next(g)
            rotate(*pend)
            for q in range(4):
                yield FV[q]
                next(g, 0)
            tgb = load_gb(I["mix_post_g"][0], fence())
            oss = AB[:, 16:32]
            st = {"lam": lam, "tlam": SHARED["tlam"], "w": qk_done, "v": v_done, "sf": {}, "tf": {}, "o": [],
                  "oss": oss, "ow": fence()}
            for q, _ in enumerate(skew(pairs([attention_a_head(h, st) for h in range(8)]), 3)):
                yield FA[q] if q < len(FA) else 0
            o_done = st["o"]
            ahead_pool()
            r, t = rstd(oss, 16, 128, o_done)
            tn = []
            for h in range(8):
                for t_ in range(2):
                    o = OA[:, t_, h * P:h * P + P]
                    tn.append(ts("pool" if t_ else "dve", o, o, r[:, 2 * h + t_:2 * h + t_ + 1], None, ALU.mult,
                                 None, [t, *o_done]))
            yield from gap(GN, True)
            th = to_halves(lambda t, k: OA[:, t, k * P:k * P + P], XTH, XTL, lambda k: AB[:, 33:34], zero,
                           [*tn, SHARED["subln"]], fence())
            ss, held = AB[:, 34:38], []
            yield from rows_linear(I["a_w_o"][0], XTH, XTL, 8, th, keep_sums(held, ss))
            xt = post_add(held, ss, tgb, X, [])
            yield from gap(1)

            def block1_ffn(layer, x_tok):
                w0 = fence()
                tgb = load_gb(I["ffn_post_g"][layer], w0)
                tn = normed(X, x_tok, YF, w0)
                yield from gap(GN, True)
                th = to_halves(lambda t, k: YF[:, t, k * P:k * P + P], XTH, XTL, gain("ffn_pre_g", 8 * layer),
                               zero, tn, w0)
                held = []

                def positions_in():
                    SHARED["pos"] = dma("pool", POS[:, :, :], I["pos"].rearrange("(t p) d -> p t d", p=P), "pos",
                                        fence())

                yield from ffn(I["ffn_w_gate_up"][layer], I["ffn_w_down"][layer], th, fence(), keep_sums(held, ss),
                               positions_in if layer == 1 else None)
                SHARED["xt"] = post_add(held, ss, tgb, X, [])
                yield from gap(1)

            yield from block1_ffn(0, xt)
            xt = SHARED["xt"]

            w0 = fence()
            tgb = load_gb(I["mix_post_g"][1], w0)
            tn = normed(X, xt, OA, w0)
            yield from gap(GN, True)
            th = to_halves(lambda t, k: OA[:, t, k * P:k * P + P], XTH, XTL, gain("kv_norm_g"), zero, tn, w0)
            qk_done, v_done = [], []
            for i in range(4):
                b, f = take()
                tk = stationary(I["kv_w"], XTH, XTL, 256 * i, b, f, th)
                dst = kT[:, 2 * i:2 * i + 2, :].rearrange("p k t -> p (k t)")
                t1 = act(dst, PS[b][:, :], ACT.Copy, [tk, *w0])
                give(b, [t1])
                qk_done.append(t1)
                yield 0
            SHARED["vw"] = w0
            yield from rows_linear(I["kv_w"], XTH, XTL, 8, th, dv, n_base=1024)
            th = to_halves(lambda t, k: OA[:, t, k * P:k * P + P], XTH, XTL, gain("mix_pre_g", 8), zero, tn,
                           fence())
            for i in range(4):
                b, f = take()
                tk = stationary(I["b_w_q"][0], XTH, XTL, 256 * i, b, f, th)
                dst = qT[:, 2 * i:2 * i + 2, :].rearrange("p k t -> p (k t)")
                t1 = act(dst, PS[b][:, :], ACT.Copy, [tk, *w0], scale=0.125)
                give(b, [t1])
                qk_done.append(t1)
                yield 0
            st = {"w": qk_done, "v": v_done, "sf": {}, "o": []}
            for q, _ in enumerate(skew(pairs([attention_b_head(h, st) for h in range(16)]), 3)):
                yield FB[q] if q < len(FB) else 0
            th = to_halves(lambda t, k: OA[:, t, k * P:k * P + P], XTH, XTL, one, zero, st["o"], fence())
            held = []
            yield from rows_linear(I["b_w_o"][0], XTH, XTL, 8, th, keep_sums(held, ss))
            xt = post_add(held, ss, tgb, X, [])
            yield from gap(1)
            yield from block1_ffn(1, xt)
            xt = SHARED["xt"]

            xt = [tt("pool" if i else "dve", X[:, i, :], X[:, i, :], POS[:, i, :], ALU.add, [SHARED["pos"], *xt])
                  for i in range(2)]

            def block2_ffn(name, w_in, w_out, v, xw):
                w0 = fence()
                sc, sh, t = modcols(name, v, 0, w0)
                if v:
                    ahead_pool()
                tn = normed(X, xw, YF, w0)
                yield from gap(GN, True)
                th = to_halves(lambda t_, k: YF[:, t_, k * P:k * P + P], XTH, XTL, sc, sh, [*tn, t], w0)
                w1 = fence()
                res = {}
                gt = []
                hs = {}
                for q, _ in enumerate(hidden(w_in, XTH, XTL, th, HTH, HTL, range(11), 0, w1, hs)):
                    yield -1 if v == 0 and q >= 22 - NH else 0
                gt = gate_rows(v + 2, 0, 0.5, GB, w0)
                for _ in rows_linear(w_out, HTH, HTL, NF, hs, gated(GB, gt, X, tn, res)):
                    yield FO if v == 0 else 0
                SHARED["xt"] = list(res.values())

            yield from block2_ffn("g_ffn1_2", I["w_ffn1_in_2"][0], I["w_ffn1_out_2"][0], 0, xt)
            xt = SHARED["xt"]

            w0 = fence()
            ahead_pool()
            tn = normed(X, xt, Hm, w0)
            yield from gap(GM, True)
            sc, sh, t = modcols("g_mix_2", 3, 0, w0)
            th = to_halves(lambda t_, k: Hm[:, t_, k * P:k * P + P], XTH, XTL, sc, sh, [*tn, t], w0)
            win = I["w_in_2"][0]
            wa = fence()
            t2 = mset("pool", mv[:, :, :, 256:257], 1.0, w0)
            lw, qw, kw, vw, late = [t2], [], [], [], []
            for _ in conv_feats(win, 0, 0, XTH, XTL, mqT, 0.0625, th, wa, None, qw):
                yield GQ
            for _ in conv_feats(win, 1024, 8, XTH, XTL, mkT, 1.0, th, wa, mk, kw, late):
                yield GQ
            for _ in values(win, XTH, XTL, th, mv, wa, vw):
                while late:
                    late.pop()()
                yield GV
            yield "drain"
            gg = gates(XTH, XTL, th, fence("main", "fill"))
            next(gg)

            def rows_to(dst, n_base, wd, res):
                def d_(tile, n0, bank, tok):
                    t1 = act(dst[:, tile, n0:n0 + 512], PS[bank][:, :], ACT.Copy, [tok, *wd])
                    give(bank, [t1])
                    res.append(t1)
                yield from rows_linear(win, XTH, XTL, 8, th, d_, n_base=n_base)

            wcf = fence("main", "fill")
            tvs, tuu, too, tga, tgb_ = [], [], [], [], []
            side = rows_to(VV, 5136, wcf, tvs)
            side2 = rows_to(UU, 4112, wcf, tuu)
            for _ in side:
                next(gg, 0)
                yield 0
            for _ in gg:
                pass
            lw += [*SHARED["gates"], *qw, *kw, *vw]
            st = {"w": lw, "h": [[], []], "su": SHARED["states"], "cs": {}, "pf": {}, "m": {}}

            def both():
                yield from side
                yield from side2
            bs = both()
            slot = iter(SS)

            def beside():
                for _ in range(next(slot, 0)):
                    next(bs, 0)

            for s_ in range(2):
                begun = [scan_start(s_, d, st) for d in range(2)]
                wu = [[], []]
                if s_ == 0:
                    wu = [mx_step(d, d, [*st["w"], *st["su"], *st["m"][d]]) for d in range(2)]
                beside()
                yield 0
                new = [[], []]
                un = [scan_head(s_, d, h, begun[d][0][h], *begun[d][1:], wu[d], new[d], st)
                      for h in range(4) for d in range(2)]
                for _ in skew(pairs(un), 3):
                    beside()
                    yield 0
                st["h"] = new
                st["su"] = [*st["su"], *wu[0], *wu[1]]
            for _ in bs:
                yield 0
            st["h"] = [*new[0], *new[1]]
            h_done = st["h"]
            w0 = fence()
            tgb = load_gb(I["g_sgu_2"][0], w0)
            tws = dma("pool", WS[:, :, :], I["w_s_2"][0].rearrange("g t s -> t g s"), "ws", w0)
            tbs = dma("pool", BSR[:, :], I["b_s_2"][0], "bs", w0)
            hn, tvs2, tuu2 = [], [], []

            def chores():
                tks = []
                for t_ in range(2):
                    tvs2.append(act(VV[:, t_, :], VV[:, t_, :], ACT.Gelu_apprx_tanh, tvs))
                    for h in range(4):
                        i = 4 * t_ + h
                        o1, o2 = bst[:, 6 * i:6 * i + 6], bag[:, 2 * i:2 * i + 2]
                        src = Hm[:, t_, 256 * h:256 * h + 256]
                        t1 = op("dve", lambda g, o1=o1, src=src: g.bn_stats(o1, src), h_done)
                        tks.append(op("dve", lambda g, o1=o1, o2=o2: g.bn_aggr(o2, o1), [t1]))
                    yield 0
                bv = bag[:, 0:16].rearrange("p (i z) -> p i z", z=2)
                var = sm(8)
                tv = cp("dve", var, bv[:, :, 1], tks)
                r, t = rstd(var, 8, 1, [tv])
                tuu2.append(act(UU[:, 0, :], UU[:, 0, :], ACT.Gelu_apprx_tanh, tuu))
                yield 0
                for t_ in range(2):
                    for h in range(4):
                        i = 4 * t_ + h
                        o = Hm[:, t_, 256 * h:256 * h + 256]
                        hn.append(ts("dve", o, o, bag[:, 2 * i:2 * i + 1], r[:, i:i + 1], ALU.subtract, ALU.mult,
                                     [t]))
                tuu2.append(act(UU[:, 1, :], UU[:, 1, :], ACT.Gelu_apprx_tanh, tuu))
                yield 0

            ch = chores()
            for _ in rows_to(OO, 3088, w0, too):
                next(ch)
                yield 0

            def spatial():
                b, f = take()
                for g2 in range(4):
                    tk = tr(PS[b][:, g2 * P:g2 * P + P], WS[:, g2, :], [tws, *f], 1 if g2 == 3 else 0)
                t1 = act(WST[:, :, :].rearrange("p g t -> p (g t)"), PS[b][:, :], ACT.Copy, [tk, *w0])
                give(b, [t1])
                b, f = take()
                tk = tr(PS[b][:, 0:4], BSR[:, :], [tbs, *f], 1)
                t2 = cp("dve", BSC[:, :], PS[b][:, 0:4], [tk, *w0])
                give(b, [t2])
                ssq, s2 = sm(4), sm(2)
                t3s = []
                for t_ in range(2):
                    for hf in range(2):
                        i_, tm, fr = tmp()
                        vs_ = VV[:, t_, 512 * hf:512 * hf + 512]
                        t3 = dot(ssq[:, 2 * hf + t_:2 * hf + t_ + 1], tm[:, :], vs_, vs_, [*tvs2, *fr])
                        TMF[i_] = [t3]
                        t3s.append(t3)
                t3 = tt("dve", s2, ssq[:, 0:2], ssq[:, 2:4], ALU.add, t3s)
                r2_, t = rstd(s2, 2, D, [t3])
                vn = [stt(VV[:, t_, :], VV[:, t_, :], r2_[:, t_:t_ + 1], GB[:, :], ALU.mult, ALU.mult, [t, tgb])
                      for t_ in range(2)]
                yield 0
                for t_ in range(2):
                    for g2 in range(2):
                        b, f = take()
                        for gg_ in range(2):
                            gi = 2 * g2 + gg_
                            tk = mm(PS[b][:, gg_ * 256:gg_ * 256 + 256], WST[:, gi, :],
                                    VV[:, t_, gi * 256:gi * 256 + 256], True, True, [t1, *vn, *f], 1 if gg_ else 0)
                        for gg_ in range(2):
                            gi = 2 * g2 + gg_
                            uo = UU[:, t_, gi * 256:gi * 256 + 256]
                            t4 = stt(uo, PS[b][:, gg_ * 256:gg_ * 256 + 256], BSC[:, gi:gi + 1], uo, ALU.add,
                                     ALU.mult, [tk, t2, *tuu2])
                            SHARED["yb"].append(t4)
                        give(b, [t4])
                    yield 0
                SHARED["thb"] = to_halves(lambda t_, k: UU[:, t_, k * P:k * P + P], XUH, XUL, one, zero,
                                          SHARED["yb"], w0)
                yield 0

            SHARED["yb"] = []
            sp_ = spatial()
            for _ in rows_to(GAA, 6160, w0, tga):
                next(sp_, 0)
                yield 0
            for _ in rows_to(GBB, 7184, w0, tgb_):
                next(sp_, 0)
                yield 0
            for _ in sp_:
                pass
            so = [act(OO[:, t_, :], OO[:, t_, :], ACT.Sigmoid, too) for t_ in range(2)]
            ya = [tt("dve" if t_ else "pool", Hm[:, t_, :], Hm[:, t_, :], OO[:, t_, :], ALU.mult, [*so, *hn])
                  for t_ in range(2)]
            sb_ = [act(GBB[:, t_, :], GBB[:, t_, :], ACT.Sigmoid, tgb_) for t_ in range(2)]
            sa_ = [act(GAA[:, t_, :], GAA[:, t_, :], ACT.Sigmoid, tga) for t_ in range(2)]
            res = {}

            def db(tile, n0, bank, tok):
                g1 = GBB[:, tile, n0:n0 + 512]
                t1 = tt("dve", g1, PS[bank][:, :], g1, ALU.mult, [tok, *sb_])
                give(bank, [t1])
                res[(tile, n0)] = t1

            w1 = fence()
            gb_ = rows_linear(I["w_branch_b_2"][0], XUH, XUL, 8, SHARED["thb"], db)
            next(gb_)
            yield 0
            th = to_halves(lambda t_, k: Hm[:, t_, k * P:k * P + P], XTH, XTL, gain("g_head_2"), zero, ya, w1)
            yield from gb_

            def da(tile, n0, bank, tok):
                g1, g2 = GAA[:, tile, n0:n0 + 512], GBB[:, tile, n0:n0 + 512]
                t1 = tt("dve", g1, PS[bank][:, :], g1, ALU.mult, [tok, *sa_])
                give(bank, [t1])
                res[(tile, n0)] = tt("dve", g2, g2, g1, ALU.add, [t1, res[(tile, n0)]])

            wb = fence()
            gt = []
            thm = {}

            def mixed_halves(half):
                w = [res[(t_, 512 * half)] for t_ in range(2)]
                thm.update(to_halves(lambda t_, k: GBB[:, t_, k * P:k * P + P], XUH, XUL, one, zero, w, wb,
                                     range(4 * half, 4 * half + 4, 2)))

            for q, _ in enumerate(rows_linear(I["w_branch_a_2"][0], XTH, XTL, 8, th, da)):
                if q == 1:
                    gt += gate_rows(5, 0, 1.0, GB, fence())
                if q == 2:
                    mixed_halves(0)
                yield 0
            res2 = {}
            go = rows_linear(I["w_out_2"][0], XUH, XUL, 8, thm, gated(GB, gt, X, [], res2))
            next(go)
            mixed_halves(1)
            yield 0
            yield from go
            res = res2
            tgf = dma("pool", XC[:, 0, :], I["g_final_2"].partition_broadcast(P), "gf", fence("main", "fill"))
            yield from block2_ffn("g_ffn2_2", I["w_ffn2_in_2"][0], I["w_ffn2_out_2"][0], 6, list(res.values()))
            xt = SHARED["xt"]
            w0 = fence()
            ss = sm(2)
            t1 = dot(ss[:, 0:1], YF[:, 0, :], X[:, 0, :], X[:, 0, :], [*xt, *w0])
            t2 = act(YF[:, 1, :], X[:, 1, :], ACT.Square, [*xt, *w0], acc=ss[:, 1:2])
            txg = tt("pool", XC[:, 1, :], X[:, 1, :], XC[:, 0, :], ALU.mult, [*xt, tgf])
            r, t = rstd(ss, 2, D, [t1, t2])
            t1 = stt(YF[:, 0, :], X[:, 0, :], r[:, 0:1], XC[:, 0, :], ALU.mult, ALU.mult, [t, tgf])
            to = dma("sp", out[0, 0:P, :], YF[:, 0, :], "out", [t1])
            for a, b in ((0, 512), (512, 1024)):
                t1 = act(YF[:, 1, a:b], XC[:, 1, a:b], ACT.Copy, [t, txg], scale=r[:, 1:2])
                to = dma("sp", out[0, P:2 * P, a:b], YF[:, 1, a:b], "out", [t1])
            Q["sp"].append((None, sems["out"], to[1]))

        GN = 2
        NH = 1
        SS = [1, 1, 0, 0, 0, 0, 1, 1, 1, 0, 0, 0, 0, 0]
        GV = -2
        GM = 4
        FO = -1
        GQ = -1
        FQ = [1, -1, -1, -1, -1, -1, -1, -1]
        FV = [-1, -1, -1, 0]
        FA = [1, 1, 1, 1, 1, 1, 1, 1]
        FB = [1, 1, 1, 1, 1, 1, 0, 1, 1, 1, 1, 1]

        def small_vectors(tl, tcg, tz2):
            for i in range(2):
                t = act(cT[:, :, i], CG[:, 144 + 8 * i:152 + 8 * i], ACT.Silu, [tcg, tz2])
            SHARED["ct"] = t
            sl, el, lam = sm(2), sm(2), AB[:, 32:33]
            i_, tm, fr = tmp()
            ta = dot(sl[:, 0:1], tm[:, 0:64], LV[:, 0:64], LV[:, 64:128], [tl, *fr])
            tb = dot(sl[:, 1:2], tm[:, 64:128], LV[:, 128:192], LV[:, 192:256], [tl])
            TMF[i_] = [ta, tb]
            ta = act(el, sl, ACT.Exp, [ta, tb])
            tlam = stt(lam, el[:, 1:2], -1.0, el[:, 0:1], ALU.mult, ALU.add, [ta])
            SHARED["tlam"] = ts("dve", lam, lam, 0.8 - 0.6, None, ALU.add, None, [tlam])
            SHARED["lvdone"] = [ta, tb, tcg, t]
            SHARED["subln"] = ts("dve", AB[:, 33:34], col("a_subln_g"), 1.0 - (0.8 - 0.6), None, ALU.mult, None,
                                 [tcg])

        def build(known):
            reset()
            stream_reset(known)
            BANKS[:] = [(i, []) for i in range(8)]
            TMF.clear()
            SGF.clear()
            SHARED.clear()
            sgi[0] = tmi[0] = smc[0] = 0
            SHARED["x"] = dma("sp", X[:, :, :], I["x"][0].rearrange("(t p) d -> p t d", p=P), "x")
            tc = dma("sp", C[:, 0:P], I["cst"][:, 0:P], "cst")
            tz = mset("pool", VR[:, :, :], 0.0)
            tz2 = mset("pool", cT[:, :, :], 0.0)
            for q, n in enumerate(sorted(VEC, key=lambda n: not n.startswith("c_"))):
                o, k = VEC[n]
                s, o = o // 128, o % 128
                v = I[n]
                if len(v.shape) == 1:
                    src = v.rearrange("(a b) -> a b", b=P)
                elif len(v.shape) == 2:
                    src = v.rearrange("l (a b) -> (l a) b", b=P)
                else:
                    src = v.rearrange("l w (a b) -> (l w a) b", b=P)
                tv = dma("sp" if q < 6 else "act", VR[o:o + k, s, :], src, "vec", [tz])
            for i, n in enumerate(["a_lambda_q1", "a_lambda_k1", "a_lambda_q2", "a_lambda_k2"]):
                tl = dma("pool", LV[:, 64 * i:64 * i + 64], I[n][0].partition_broadcast(P), "lam")
            SHARED["rot"] = dma("pool", GB[:, 0:2 * T], I["cst"][:, CK:CW], "gb")
            SHARED["ba"] = dma("pool", BA[:, :], I["b_ada_2"].rearrange("l (a b) -> (l a) b", b=512), "ba")
            tc2 = dma("act", C[:, P:CK], I["cst"][:, P:CK], "cst2")
            if known is not None:
                pump()
            SHARED["tn"] = normed(X, [SHARED["x"]], OA, [], "dve")
            b, f = take()
            tr(PS[b][:, 0:128], VR[:, 0, :], [tc, tv, *f])
            tk = tr(PS[b][:, 128:160], VR[0:NV2, 1, :], (), 1)
            tcg = SHARED["cg"] = act(CG[:, :], PS[b][:, 0:160], ACT.Copy, [tk])
            give(b, [tcg])
            SHARED["cst"] = tc2
            SHARED["small"] = lambda: small_vectors(tl, tcg, tz2)
            SHARED["mods"] = []
            SHARED["ada"] = ada_steps()
            fill = context_stream()

            def step():
                who_emits[0] = "fill"
                r = next(fill, "end")
                who_emits[0] = "main"
                return r != "end"

            n = 0
            for want in main_stream():
                if want == "drain":
                    while "states" not in SHARED:
                        step()
                    continue
                if want < 0:
                    for _ in range(-want):
                        step()
                    continue
                goal = ST["got"] + want
                while ST["got"] < goal and step():
                    pass
                n += want == 0
                if want == 0 and n % ADA_EVERY == 0:
                    who_emits[0] = "fill"
                    next(SHARED["ada"], 0)
                    who_emits[0] = "main"
            while step():
                pass

        ADA_EVERY = 6
        build(None)
        build(list(plan))

        block = ctx.enter_context(nc.Block())

        def play(eng, items):
            for f, s, v in items:
                if f is None:
                    eng.wait_ge(s, v)
                else:
                    i = f(eng)
                    if s is not None:
                        i.then_inc(s, v)

        @block.sync
        def _(eng):
            play(eng, Q["sp"])

        @block.tensor
        def _(eng):
            play(eng, Q["pe"])

        @block.scalar
        def _(eng):
            play(eng, Q["act"])

        @block.vector
        def _(eng):
            play(eng, Q["dve"])

        @block.gpsimd
        def _(eng):
            play(eng, Q["pool"])


_INS = [
    "x", "a_w_qkv", "a_w_o", "a_lambda_q1", "a_lambda_k1", "a_lambda_q2", "a_lambda_k2", "a_subln_g", "kv_norm_g",
    "kv_w", "b_w_q", "b_w_o", "mix_pre_g", "mix_post_g", "ffn_pre_g", "ffn_post_g", "ffn_w_gate_up", "ffn_w_down",
    "c_2", "ctx_2", "c_ctx_2", "w_ada_2", "b_ada_2", "g_ffn1_2", "w_ffn1_in_2", "w_ffn1_out_2", "g_mix_2", "w_in_2",
    "b_gates_2", "conv_qk_w_2", "conv_qk_b_2", "g_head_2", "g_sgu_2", "w_s_2", "b_s_2", "w_branch_a_2",
    "w_branch_b_2", "w_out_2", "g_ffn2_2", "w_ffn2_in_2", "w_ffn2_out_2", "g_final_2",
]


def kernel(**inputs):
    import numpy as _np
    import concourse.bacc as _bacc
    from concourse import mybir as _mybir
    from concourse.bass_utils import run_bass_kernel_spmd as _run

    nc = _bacc.Bacc("TRN2", target_bir_lowering=False, num_devices=1)
    arrays, args = {}, {}
    for name in _INS:
        arrays[name] = _np.ascontiguousarray(inputs[name])
    arrays["cst"] = constants()
    arrays["pos"] = positions()
    ins = {}
    for name, a in arrays.items():
        ins[f"in_{name}_dram"] = a
        args[name] = nc.dram_tensor(f"in_{name}_dram", a.shape, _mybir.dt.from_np(a.dtype), kind="ExternalInput").ap()
    out = nc.dram_tensor("out_0_dram", (1, 256, 1024), _mybir.dt.float32, kind="ExternalOutput").ap()
    program(nc, args, out)
    r = _run(nc, [ins], core_ids=[0])
    return r.results[0]["out_0_dram"]
```
